# Optimizing a Trainium2 kernel written in Bass

```python
import math
import jax
import jax.numpy as jnp
from jax import lax
import numpy as np

D_MODEL = 1024
BATCH = 1
SEQ = 256
DEPTH = 2

MEM_LEN = 256
NORM_EPS = 1e-6
SWA_Q_HEADS = 8
SWA_KV_HEADS = 2
SWA_HEAD_DIM = 64
SWA_WINDOW = 128
SWA_BLOCK = 128
ROPE_THETA = 150000.0
MOBA_HEADS = 8
MOBA_HEAD_DIM = 64
MOBA_BLOCK = 256
MOBA_TOPK = 3
MOBA_Q_CHUNK = 64
SSD_D_INNER = D_MODEL
SSD_HEAD_DIM = 64
SSD_HEADS = SSD_D_INNER // SSD_HEAD_DIM
SSD_GROUPS = 2
SSD_D_STATE = 128
SSD_CONV = 4
SSD_CHUNK = 128
DT_MIN = 0.001
DT_MAX = 0.1
X_HEADS = 4
X_HEAD_DIM = D_MODEL // X_HEADS
D_FF = 4 * D_MODEL
N_BRANCH = 3

SWA_Q_W = SWA_Q_HEADS * SWA_HEAD_DIM
SWA_KV_W = SWA_KV_HEADS * SWA_HEAD_DIM
MOBA_W = MOBA_HEADS * MOBA_HEAD_DIM
SSD_BC_W = SSD_GROUPS * SSD_D_STATE
SSD_XBC_W = SSD_D_INNER + 2 * SSD_BC_W
IN_SIZES = (SWA_Q_W, SWA_KV_W, SWA_KV_W, MOBA_W, MOBA_W, MOBA_W, SSD_D_INNER, SSD_XBC_W, SSD_HEADS)
D_IN_PROJ = sum(IN_SIZES)

kernel_name = 'hybrid_swa_moba_ssd_gated_block'

def split_cols(t, sizes):
    cuts, acc = [], 0
    for s in sizes[:-1]:
        acc += s
        cuts.append(acc)
    return jnp.split(t, cuts, axis=-1)

def rmsnorm(x, w):
    xf = x.astype(jnp.float32)
    y = xf * lax.rsqrt(jnp.mean(xf * xf, axis=-1, keepdims=True) + NORM_EPS)
    return (y * w.astype(jnp.float32)).astype(x.dtype)

def apply_rope(t, positions):
    half = t.shape[-1] // 2
    inv = ROPE_THETA ** (-jnp.arange(half, dtype=jnp.float32) / half)
    ang = positions.astype(jnp.float32)[..., None] * inv
    cos = jnp.cos(ang)[:, :, None, :]
    sin = jnp.sin(ang)[:, :, None, :]
    tf = t.astype(jnp.float32)
    t1, t2 = tf[..., :half], tf[..., half:]
    return jnp.concatenate([t1 * cos - t2 * sin, t2 * cos + t1 * sin], axis=-1).astype(t.dtype)

def swa_sink_attention(q, k, v, sinks):
    B, S, _, hd = q.shape
    nb = S // SWA_BLOCK
    G = SWA_Q_HEADS // SWA_KV_HEADS
    qb = q.reshape(B, nb, SWA_BLOCK, SWA_KV_HEADS, G, hd)

    def bands(t):
        tp = jnp.pad(t, ((0, 0), (SWA_BLOCK, 0), (0, 0), (0, 0)))
        tp = tp.reshape(B, nb + 1, SWA_BLOCK, SWA_KV_HEADS, hd)
        return jnp.concatenate([tp[:, :-1], tp[:, 1:]], axis=2)

    kb, vb = bands(k), bands(v)
    s = jnp.einsum('bnqkgd,bnskd->bnkgqs', qb, kb).astype(jnp.float32) * (hd ** -0.5)
    qi = jnp.arange(SWA_BLOCK)[:, None] + SWA_BLOCK
    si = jnp.arange(2 * SWA_BLOCK)[None, :]
    delta = qi - si
    kpos = jnp.arange(nb)[:, None, None] * SWA_BLOCK - SWA_BLOCK + si[None]
    mask = (delta >= 0)[None] & (delta < SWA_WINDOW)[None] & (kpos >= 0)
    s = jnp.where(mask[None, :, None, None], s, -jnp.inf)
    sink = sinks.astype(jnp.float32).reshape(SWA_KV_HEADS, G)[None, None, :, :, None, None]
    m = jnp.maximum(jnp.max(s, axis=-1, keepdims=True), sink)
    p = jnp.exp(s - m)
    denom = jnp.sum(p, axis=-1, keepdims=True) + jnp.exp(sink - m)
    o = jnp.einsum('bnkgqs,bnskd->bnqkgd', (p / denom).astype(v.dtype), vb)
    return o.reshape(B, S, SWA_Q_HEADS * hd)

def moba_attention(q, k, v):
    B, S, H, hd = q.shape
    nkb = -(-S // MOBA_BLOCK)
    pad = nkb * MOBA_BLOCK - S
    scale = hd ** -0.5
    qh = jnp.transpose(q, (0, 2, 1, 3))

    def blocks(t):
        t = jnp.pad(jnp.transpose(t, (0, 2, 1, 3)), ((0, 0), (0, 0), (0, pad), (0, 0)))
        return t.reshape(B, H, nkb, MOBA_BLOCK, hd)

    kb, vb = blocks(k), blocks(v)
    k_mean = jnp.mean(kb.astype(jnp.float32), axis=3)
    topk = min(MOBA_TOPK, nkb)
    b_idx = jnp.arange(B)[:, None, None, None]
    h_idx = jnp.arange(H)[None, :, None, None]
    blk_ids = jnp.arange(nkb)
    n_sel = topk * MOBA_BLOCK

    def chunk(c):
        start = c * MOBA_Q_CHUNK
        qs = lax.dynamic_slice_in_dim(qh, start, MOBA_Q_CHUNK, axis=2)
        qpos = start + jnp.arange(MOBA_Q_CHUNK)
        own = start // MOBA_BLOCK
        gate = jnp.einsum('bhqd,bhnd->bhqn', qs.astype(jnp.float32), k_mean)
        gate = jnp.where(blk_ids < own, gate, -jnp.inf)
        _, sel = lax.top_k(gate, topk)
        sel_ok = sel < own
        kg = kb[b_idx, h_idx, sel]
        vg = vb[b_idx, h_idx, sel]
        s_sel = jnp.einsum('bhqd,bhqksd->bhqks', qs, kg).astype(jnp.float32) * scale
        s_sel = jnp.where(sel_ok[..., None], s_sel, -jnp.inf).reshape(B, H, MOBA_Q_CHUNK, n_sel)
        k_own = lax.dynamic_index_in_dim(kb, own, axis=2, keepdims=False)
        v_own = lax.dynamic_index_in_dim(vb, own, axis=2, keepdims=False)
        s_own = jnp.einsum('bhqd,bhsd->bhqs', qs, k_own).astype(jnp.float32) * scale
        kpos = own * MOBA_BLOCK + jnp.arange(MOBA_BLOCK)
        s_own = jnp.where(kpos[None, :] <= qpos[:, None], s_own, -jnp.inf)
        p = jax.nn.softmax(jnp.concatenate([s_sel, s_own], axis=-1), axis=-1).astype(v.dtype)
        p_sel = p[..., :n_sel].reshape(B, H, MOBA_Q_CHUNK, topk, MOBA_BLOCK)
        p_own = p[..., n_sel:]
        return (jnp.einsum('bhqks,bhqksd->bhqd', p_sel, vg)
                + jnp.einsum('bhqs,bhsd->bhqd', p_own, v_own))

    out = lax.map(chunk, jnp.arange(S // MOBA_Q_CHUNK))
    return jnp.transpose(out, (1, 0, 3, 2, 4)).reshape(B, S, H * hd)

def causal_depthwise_conv(t, w, b):
    y = lax.conv_general_dilated(t, w[:, None, :], window_strides=(1,), padding=[(SSD_CONV - 1, 0)],
                                 dimension_numbers=('NWC', 'WIO', 'NWC'), feature_group_count=t.shape[-1])
    return y + b

def segsum_exp(a_cs):
    L = a_cs.shape[-1]
    diff = a_cs[..., :, None] - a_cs[..., None, :]
    mask = jnp.tril(jnp.ones((L, L), dtype=bool))
    return jnp.exp(jnp.where(mask, diff, -jnp.inf))

def ssd_scan(xh, dt, a, bm, cm):
    B, S, H, P = xh.shape
    G, N = bm.shape[2], bm.shape[3]
    R = H // G
    L = SSD_CHUNK
    nc = S // L
    x_ = (xh.astype(jnp.float32) * dt[..., None]).reshape(B, nc, L, G, R, P)
    a_ = jnp.transpose((dt * a).reshape(B, nc, L, G, R), (0, 3, 4, 1, 2))
    a_cs = jnp.cumsum(a_, axis=-1)
    b_ = bm.astype(jnp.float32).reshape(B, nc, L, G, N)
    c_ = cm.astype(jnp.float32).reshape(B, nc, L, G, N)
    cb = jnp.einsum('bclgn,bcsgn->bgcls', c_, b_)
    wmat = cb[:, :, None] * segsum_exp(a_cs)
    y_diag = jnp.einsum('bgrcls,bcsgrp->bclgrp', wmat, x_)
    decay_states = jnp.exp(a_cs[..., -1:] - a_cs)
    states = jnp.einsum('bclgn,bgrcl,bclgrp->bcgrpn', b_, decay_states, x_)
    chunk_decay = jnp.exp(a_cs[..., -1])

    def step(h, inp):
        st, dec = inp
        return h * dec[..., None, None] + st, h

    h0 = jnp.zeros((B, G, R, P, N), jnp.float32)
    _, prev = lax.scan(step, h0, (jnp.moveaxis(states, 1, 0), jnp.moveaxis(chunk_decay, 3, 0)))
    y_off = jnp.einsum('bclgn,cbgrpn,bgrcl->bclgrp', c_, prev, jnp.exp(a_cs))
    return (y_diag + y_off).reshape(B, S, H, P)

def ssd_mixer(z, xbc, dt_raw, conv_w, conv_b, dt_bias, a_log, d_skip, norm_w):
    B, S, _ = z.shape
    xbc = jax.nn.silu(causal_depthwise_conv(xbc, conv_w, conv_b))
    xs, bm, cm = split_cols(xbc, (SSD_D_INNER, SSD_BC_W, SSD_BC_W))
    xh = xs.reshape(B, S, SSD_HEADS, SSD_HEAD_DIM)
    bm = bm.reshape(B, S, SSD_GROUPS, SSD_D_STATE)
    cm = cm.reshape(B, S, SSD_GROUPS, SSD_D_STATE)
    dt = jax.nn.softplus(dt_raw.astype(jnp.float32) + dt_bias.astype(jnp.float32))
    a = -jnp.exp(a_log.astype(jnp.float32))
    y = ssd_scan(xh, dt, a, bm, cm) + xh.astype(jnp.float32) * d_skip.astype(jnp.float32)[:, None]
    y = y.reshape(B, S, SSD_D_INNER) * jax.nn.silu(z.astype(jnp.float32))
    yg = y.reshape(B, S, SSD_GROUPS, SSD_D_INNER // SSD_GROUPS)
    yg = yg * lax.rsqrt(jnp.mean(yg * yg, axis=-1, keepdims=True) + NORM_EPS)
    return (yg.reshape(B, S, SSD_D_INNER) * norm_w.astype(jnp.float32)).astype(z.dtype)

def hybrid_layer(x, mem, positions, norm_mix, w_in, w_gate, b_gate, swa_sinks, conv_w, conv_b,
                 dt_bias, a_log, d_skip, ssd_norm, w_br_swa, w_br_moba, w_br_ssd, w_mix_out,
                 norm_cross, norm_mem, w_cq, w_ckv, w_co, norm_mlp, w_up, w_down):
    B, S, D = x.shape
    h = rmsnorm(x, norm_mix)
    q_a, k_a, v_a, q_b, k_b, v_b, z, xbc, dt_raw = split_cols(h @ w_in, IN_SIZES)
    q_a = apply_rope(q_a.reshape(B, S, SWA_Q_HEADS, SWA_HEAD_DIM), positions)
    k_a = apply_rope(k_a.reshape(B, S, SWA_KV_HEADS, SWA_HEAD_DIM), positions)
    v_a = v_a.reshape(B, S, SWA_KV_HEADS, SWA_HEAD_DIM)
    y_a = swa_sink_attention(q_a, k_a, v_a, swa_sinks)
    y_b = moba_attention(q_b.reshape(B, S, MOBA_HEADS, MOBA_HEAD_DIM),
                         k_b.reshape(B, S, MOBA_HEADS, MOBA_HEAD_DIM),
                         v_b.reshape(B, S, MOBA_HEADS, MOBA_HEAD_DIM))
    y_c = ssd_mixer(z, xbc, dt_raw, conv_w, conv_b, dt_bias, a_log, d_skip, ssd_norm)
    gates = jax.nn.sigmoid((h @ w_gate + b_gate).astype(jnp.float32)).astype(x.dtype)
    g_a, g_b, g_c = jnp.split(gates, N_BRANCH, axis=-1)
    merged = g_a * (y_a @ w_br_swa) + g_b * (y_b @ w_br_moba) + g_c * (y_c @ w_br_ssd)
    x = x + merged @ w_mix_out
    hq = rmsnorm(x, norm_cross)
    hm = rmsnorm(mem, norm_mem)
    q = (hq @ w_cq).reshape(B, S, X_HEADS, X_HEAD_DIM)
    k, v = jnp.split(hm @ w_ckv, 2, axis=-1)
    k = k.reshape(B, MEM_LEN, X_HEADS, X_HEAD_DIM)
    v = v.reshape(B, MEM_LEN, X_HEADS, X_HEAD_DIM)
    s = jnp.einsum('bshd,bmhd->bhsm', q, k).astype(jnp.float32) * (X_HEAD_DIM ** -0.5)
    p = jax.nn.softmax(s, axis=-1).astype(v.dtype)
    o = jnp.einsum('bhsm,bmhd->bshd', p, v).reshape(B, S, D)
    x = x + o @ w_co
    hf = rmsnorm(x, norm_mlp)
    return x + jnp.square(jax.nn.relu(hf @ w_up)) @ w_down

def setup_inputs(seed: int = 0) -> dict:
    key = jax.random.key(seed)
    ks = jax.random.split(key, 32)
    f32 = jnp.float32
    D = D_MODEL

    def dense(k, shape, fan_in):
        return jax.random.normal(k, shape, f32) * (fan_in ** -0.5)

    def gain(k, shape):
        return 1.0 + 0.05 * jax.random.normal(k, shape, f32)

    def small(k, shape):
        return 0.01 * jax.random.normal(k, shape, f32)

    dt0 = jnp.exp(jax.random.uniform(ks[9], (DEPTH, SSD_HEADS), f32, math.log(DT_MIN), math.log(DT_MAX)))
    return {
        'x': jax.random.normal(ks[0], (BATCH, SEQ, D), f32),
        'mem': jax.random.normal(ks[1], (BATCH, MEM_LEN, D), f32),
        'positions': jnp.broadcast_to(jnp.arange(SEQ, dtype=jnp.int32)[None, :], (BATCH, SEQ)),
        'norm_mix': gain(ks[2], (DEPTH, D)),
        'w_in': dense(ks[3], (DEPTH, D, D_IN_PROJ), D),
        'w_gate': dense(ks[4], (DEPTH, D, N_BRANCH * D), D),
        'b_gate': small(ks[5], (DEPTH, N_BRANCH * D)),
        'swa_sinks': jax.random.normal(ks[6], (DEPTH, SWA_Q_HEADS), f32),
        'conv_w': dense(ks[7], (DEPTH, SSD_CONV, SSD_XBC_W), SSD_CONV),
        'conv_b': small(ks[8], (DEPTH, SSD_XBC_W)),
        'dt_bias': dt0 + jnp.log(-jnp.expm1(-dt0)),
        'a_log': jnp.log(jax.random.uniform(ks[10], (DEPTH, SSD_HEADS), f32, 1.0, 16.0)),
        'd_skip': gain(ks[11], (DEPTH, SSD_HEADS)),
        'ssd_norm': gain(ks[12], (DEPTH, SSD_D_INNER)),
        'w_br_swa': dense(ks[13], (DEPTH, SWA_Q_W, D), SWA_Q_W),
        'w_br_moba': dense(ks[14], (DEPTH, MOBA_W, D), MOBA_W),
        'w_br_ssd': dense(ks[15], (DEPTH, SSD_D_INNER, D), SSD_D_INNER),
        'w_mix_out': dense(ks[16], (DEPTH, D, D), D),
        'norm_cross': gain(ks[17], (DEPTH, D)),
        'norm_mem': gain(ks[18], (DEPTH, D)),
        'w_cq': dense(ks[19], (DEPTH, D, D), D),
        'w_ckv': dense(ks[20], (DEPTH, D, 2 * D), D),
        'w_co': dense(ks[21], (DEPTH, D, D), D),
        'norm_mlp': gain(ks[22], (DEPTH, D)),
        'w_up': dense(ks[23], (DEPTH, D, D_FF), D),
        'w_down': dense(ks[24], (DEPTH, D_FF, D), D_FF),
        'final_norm': gain(ks[25], (D,)),
    }

def reference(x, mem, positions, norm_mix, w_in, w_gate, b_gate, swa_sinks, conv_w, conv_b,
              dt_bias, a_log, d_skip, ssd_norm, w_br_swa, w_br_moba, w_br_ssd, w_mix_out,
              norm_cross, norm_mem, w_cq, w_ckv, w_co, norm_mlp, w_up, w_down, final_norm):
    for l in range(DEPTH):
        x = hybrid_layer(x, mem, positions, norm_mix[l], w_in[l], w_gate[l], b_gate[l], swa_sinks[l],
                         conv_w[l], conv_b[l], dt_bias[l], a_log[l], d_skip[l], ssd_norm[l],
                         w_br_swa[l], w_br_moba[l], w_br_ssd[l], w_mix_out[l], norm_cross[l],
                         norm_mem[l], w_cq[l], w_ckv[l], w_co[l], norm_mlp[l], w_up[l], w_down[l])
    return rmsnorm(x, final_norm)


_drawn_inputs = setup_inputs


def setup_inputs(seed=0):
    import zlib

    import numpy as np

    out = dict(_drawn_inputs(seed))
    spreads = {}
    factors = {'b_gate': 8.0, 'swa_sinks': 4.602, 'conv_b': 6.422, 'norm_cross': 8.0, 'norm_mem': 6.13}
    for name, (base, spread) in spreads.items():
        noise = np.random.default_rng([zlib.crc32(name.encode()), seed]).standard_normal(out[name].shape)
        drawn = base * np.exp(spread * noise) if base else spread * noise
        out[name] = jnp.asarray(drawn.astype(out[name].dtype))
    for name, factor in factors.items():
        out[name] = (out[name] * factor).astype(out[name].dtype)
    return out
```

```python
import math
from contextlib import ExitStack

import numpy as np
import concourse.bass as bass
from concourse import mybir

F32 = mybir.dt.float32
F32R = mybir.dt.float32r
I32 = mybir.dt.int32
ALU = mybir.AluOpType
ACT = mybir.ActivationFunctionType
AX = mybir.AxisListType

P = 128
D = 1024
SEQ = 256
DEPTH = 2
KT = D // P
TT = SEQ // P
EPS = 1e-6
HD = 64
HEADS = 8
SWA_KV = 2
SSD_HEADS = 16
SSD_GROUPS = 2
ROPE_THETA = 150000.0
X_HEADS = 4
D_FF = 4 * D
FF_BLOCKS = D_FF // 512
NEG = -1.0e30
ATT_SCALE = HD ** -0.5
X_SCALE = (D // X_HEADS) ** -0.5

C_QA, C_KVA, C_QB, C_KB, C_VB, C_Z, C_XBC, C_DT = 0, 512, 768, 1280, 1792, 2304, 3328, 4864

PC_NORM = [0, 16, 8, 24]
PC_SSDN, PC_CONVW, PC_CONVB, PC_BGATE, PC_ROWS = 32, 40, 88, 100, 124
PC_DTB, PC_NEGA, PC_DSKIP, PC_SINK, PC_ALL = 124, 140, 156, 172, 180

RING = 3


def make_units():
    units = []

    def unit(kind, orient, weight, row, k_tiles, col, cols, act, index, first=True, last=True):
        units.append(dict(kind=kind, orient=orient, weight=weight, row=row, kt=k_tiles, col=col, cols=cols,
                          act=act, index=index, first=first, last=last))

    def stripes_b(kind, weight, col, act, n):
        for j in range(n):
            for half in range(2):
                unit(kind, "B", weight, 512 * half, 4, col + 512 * j, 512, act, j, half == 0, half == 1)

    def stripes_a(kind, weight, col, act, n):
        for j in range(n):
            unit(kind, "A", weight, 0, 8, col + 256 * j, 256, act, j)

    stripes_b("qa", "w_in", C_QA, "h", 1)
    unit("kva", "B", "w_in", 0, 8, C_KVA, 256, "h", 0)
    stripes_a("qkb", "w_in", C_QB, "h", 4)
    stripes_b("vb", "w_in", C_VB, "h", 1)
    unit("dt", "B", "w_in", 0, 8, C_DT, SSD_HEADS, "h", 0)
    stripes_a("xbc", "w_in", C_XBC, "h", 6)
    stripes_b("z", "w_in", C_Z, "h", 2)
    stripes_a("gate", "w_gate", 0, "h", 4)
    for j in range(2):
        unit("branch_a", "A", "w_br_swa", 0, 4, 512 * j, 512, "y_swa", j)
    stripes_a("gate", "w_gate", D, "h", 4)
    for j in range(2):
        unit("branch_b", "A", "w_br_moba", 0, 4, 512 * j, 512, "y_moba", j)
    stripes_a("gate", "w_gate", 2 * D, "h", 4)
    stripes_a("branch_c", "w_br_ssd", 0, "y_ssd", 4)
    stripes_b("mix", "w_mix_out", 0, "merged", 2)
    stripes_a("kx", "w_ckv", 0, "mem", 4)
    stripes_a("qx", "w_cq", 0, "hq", 4)
    stripes_b("vx", "w_ckv", D, "mem", 2)
    stripes_b("co", "w_co", 0, "o", 2)

    def up(f):
        for j in range(2):
            unit("up", "A", "w_up", 0, 8, 512 * f + 256 * j, 256, "hf", 2 * f + j)

    def down(f):
        for j in range(2):
            unit("down", "B", "w_down", 512 * f, 4, 512 * j, 512, "relu", 2 * f + j,
                 f == 0, f == FF_BLOCKS - 1)

    up(0)
    for f in range(FF_BLOCKS - 1):
        up(f + 1)
        down(f)
    down(FF_BLOCKS - 1)
    return units


UNITS = make_units()
NU = len(UNITS)


def first_of(kind, index=0):
    return next(u for u, w in enumerate(UNITS) if w["kind"] == kind and w["index"] == index)


U_QA, U_KVA, U_QKB, U_VB, U_DT, U_XBC, U_Z = (first_of(k) for k in ("qa", "kva", "qkb", "vb", "dt", "xbc", "z"))
U_GATE, U_BRA, U_BRB, U_BRC, U_MIX = (first_of(k) for k in ("gate", "branch_a", "branch_b", "branch_c", "mix"))
U_KX, U_QX, U_VX, U_CO, U_UP = (first_of(k) for k in ("kx", "qx", "vx", "co", "up"))

JOB_SLOT0 = 4
NJOBS = 24
SWA_T_SLOT = 3
ACS_SLOT, CB_SLOT, BTOK_SLOT, XS_SLOT, STATES_SLOT = 10, 16, 17, 18, 20
NORM_SCALE_SLOT = {1: U_MIX, 2: U_KX - 1, 3: U_UP - 1}
NORM_TURN_SLOT = {1: U_MIX + 1, 2: U_QX - 2, 3: U_UP - 1}
CROSS_SLOT0 = U_VX - 1


def job_of(n):
    return n // 8, (n % 8) // 4, n % 4


def head_of(j, i):
    return 4 * (j // 2) + j % 2 + 2 * i


CLOSINGS = [(3, 0, 0, 0), (7, 0, 1, 0), (11, 1, 0, 0), (15, 1, 1, 0),
            (17, 2, 0, 0), (19, 2, 0, 1), (21, 2, 1, 0), (23, 2, 1, 1)]
CLOSE_SLOT = [JOB_SLOT0 + c[0] + 2 for c in CLOSINGS]

SB_, TB_, OB_, YB_ = 4, 5, 6, 7


def unit_banks(u, w):
    if w["kind"] == "down":
        return [("down", 2 * (w["index"] % 2) + t) for t in range(TT)]
    if w["kind"] in ("kva", "dt"):
        return [(u, 0)]
    if w["orient"] == "B":
        return [(u if w["first"] else u - 1, t) for t in range(TT)]
    return [(u, i) for i in range(w["cols"] // 256)]


def slot_banks(s):
    out = []
    if s == SWA_T_SLOT:
        out += [(b, ("qkT", i)) for i, b in enumerate((SB_, TB_, OB_))]
    n = s - JOB_SLOT0
    if 0 <= n < NJOBS:
        out.append((SB_, ("score", n)))
    if 0 <= n - 1 < 16:
        out.append((TB_, ("probsT", n - 1)))
    if 0 <= n - 2 < NJOBS and (n - 2) in [0, 4, 8, 12, 16, 18, 20, 22]:
        out.append((OB_, ("values", n - 2)))
    if s == ACS_SLOT:
        out.append((YB_, ("acs",)))
    if s == CB_SLOT:
        out.append((YB_, ("cb",)))
    if s == BTOK_SLOT:
        out.append((YB_, ("btok",)))
    if s in (XS_SLOT, XS_SLOT + 1):
        out += [(YB_, ("xs", s - XS_SLOT, 0)), (SB_, ("xs", s - XS_SLOT, 1))]
    if s == STATES_SLOT:
        out += [(YB_, ("states", 0)), (SB_, ("states", 1))]
    for i, (_, branch, tile, group) in enumerate(CLOSINGS):
        if branch == 2 and tile == 1 and s == CLOSE_SLOT[i]:
            out.append((YB_, ("yoff", group)))
    for i in range(8):
        if s == CLOSE_SLOT[i] + 1:
            out.append((YB_, ("closeT", i)))
    for n in (1, 2, 3):
        if s == NORM_TURN_SLOT[n]:
            out += [(SB_ + b, ("norm", n, b)) for b in range(4)]
    h = s - CROSS_SLOT0
    if 0 <= h < X_HEADS:
        out.append((SB_, ("xscore", h)))
    if 0 <= h - 1 < X_HEADS:
        out.append((TB_, ("xprobsT", h - 1)))
    if s == U_VX + 2:
        out += [(OB_, ("xvalues", 0)), (YB_, ("xvalues", 1))]
    if s == U_VX + 3:
        out += [(OB_, ("xvalues", 2)), (YB_, ("xvalues", 3))]
    return out


def make_banks():
    where, uses, turn = {}, [0] * 8, 0

    def use(bank, key):
        where[key] = (bank, uses[bank])
        uses[bank] += 1

    for b in range(4):
        use(SB_ + b, ("norm", 0, b))
    for u, w in enumerate(UNITS):
        for key in unit_banks(u, w):
            if key in where:
                continue
            if w["kind"] == "down":
                use(SB_ + key[1], key)
            else:
                use(turn % 4, key)
                turn += 1
        for bank, key in slot_banks(u):
            use(bank, key)
    return where, uses


BANK_OF, BANK_USES = make_banks()
DVE_STEPS = 143


class Signal:

    def __init__(self, sem, per_layer, credit=0):
        self.sem, self.per_layer, self.credit = sem, per_layer, credit

    def at(self, l, n):
        assert n + self.credit > 0
        return self.sem, l * self.per_layer + (n + self.credit)


class Steps:

    def __init__(self, eng, sem, per_layer):
        self.eng, self.sem, self.per_layer = eng, sem, per_layer
        self.before, self.n, self.l = 0, 0, 0

    def enter(self, l):
        self.before, self.n, self.l = self.before + self.n, 0, l

    def leave(self, layers):
        assert self.n == self.per_layer, f"{self.sem}: {self.n} steps a layer"
        self.before, self.n, self.l = self.before + layers * self.n, 0, 0

    def mark(self, ins):
        ins.then_inc(self.sem, 1)
        self.n += 1

    def settle(self):
        self.eng.wait_ge(self.sem, self.l * self.per_layer + (self.before + self.n))

    def link(self, ins):
        self.mark(ins)
        self.settle()


def trunk(nc, a, out):
    ctx = ExitStack()
    with ctx:
        top = [-(-nc.sbuf_base // 64) * 64]

        def at(name, shape, dtype, offset):
            return nc.alloc_sbuf_tensor_at(name, shape, dtype, offset=offset)

        def region(n_bytes):
            offset = top[0]
            top[0] += n_bytes
            assert top[0] <= nc.sbuf_usable_end, top[0]
            return offset

        def keep(name, shape, dtype=F32):
            size = int(np.prod(shape[1:])) * 4
            return at(name, shape, dtype, region(-(-size // 32) * 32))

        raw = keep("raw", [P, RING, 2048])
        w_hi = keep("w_hi", [P, RING, 2048], F32R)
        w_lo = keep("w_lo", [P, RING, 2048], F32R)
        x_sb = keep("x_sb", [P, TT, D])
        act_hi = keep("act_hi", [P, KT, SEQ], F32R)
        act_lo = keep("act_lo", [P, KT, SEQ], F32R)

        r_a = region(8192)
        qk_tok = at("qk_tok", [P, TT, 768], F32, r_a)
        z_sb = at("z_sb", [P, TT, D], F32, r_a)
        mem_sb = at("mem_sb", [P, TT, D], F32, r_a)
        rows = at("rows", [P, DEPTH, P], F32, r_a)
        r_b = region(8192)
        qkT_a = at("qkT_a", [P, 6, SEQ], F32, r_b)
        v_a = at("v_a", [P, TT, P], F32, r_b + 6144)
        xdt = at("xdt", [P, TT, D], F32, r_b)
        v_x = at("v_x", [P, TT, D], F32, r_b)
        r_c = region(16384)
        qkT_b = at("qkT_b", [P, 8, SEQ], F32, r_c)
        v_b = at("v_b", [P, TT, 512], F32, r_c + 8192)
        yc_hi = at("yc_hi", [P, KT, SEQ], F32R, r_c)
        yc_lo = at("yc_lo", [P, KT, SEQ], F32R, r_c + 8192)
        hm_hi = at("hm_hi", [P, KT, SEQ], F32R, r_c)
        hm_lo = at("hm_lo", [P, KT, SEQ], F32R, r_c + 8192)
        r_d = region(8192)
        ya_hi = at("ya_hi", [P, 4, SEQ], F32R, r_d)
        ya_lo = at("ya_lo", [P, 4, SEQ], F32R, r_d + 4096)
        q_xT = at("q_xT", [P, KT, SEQ], F32, r_d)
        r_e = region(8192)
        yb_hi = at("yb_hi", [P, 4, SEQ], F32R, r_e)
        yb_lo = at("yb_lo", [P, 4, SEQ], F32R, r_e + 4096)
        pT_x = at("pT_x", [P, X_HEADS, TT, SEQ], F32, r_e)
        r_f = region(12288)
        xbcT = at("xbcT", [P, 12, SEQ], F32, r_f)
        xd_sb = at("xd_sb", [P, SSD_GROUPS, TT, 512], F32, r_f)
        k_xT = at("k_xT", [P, KT, SEQ], F32, r_f)
        r_g = region(16384)
        g_sb = at("g_sb", [P, KT, SEQ], F32, r_g)
        h_tok = at("h_tok", [P, TT, D], F32, r_g)
        mg_sb = at("mg_sb", [P, KT, SEQ], F32, r_g + 8192)
        gain = at("gain", [P, D], F32, r_g + 8192)
        o_hi = at("o_hi", [P, KT, SEQ], F32R, r_g)
        o_lo = at("o_lo", [P, KT, SEQ], F32R, r_g + 8192)
        relu_hi = at("relu_hi", [P, 2, 4, SEQ], F32R, r_g)
        relu_lo = at("relu_lo", [P, 2, 4, SEQ], F32R, r_g + 8192)
        s_sb = keep("s_sb", [P, 2, 512])
        pT_sb = keep("pT_sb", [P, 2, 512])
        y_tok = keep("y_tok", [P, 512])
        tmp = keep("tmp", [P, 2, 512])
        xdec = keep("xdec", [P, D])
        states = keep("states", [P, SSD_GROUPS, 512])
        cbT = keep("cbT", [P, TT * SSD_GROUPS, P])
        b_tok = keep("b_tok", [P, SSD_GROUPS, P])

        ident = keep("ident", [P, P])
        tri = keep("tri", [P, P])
        ones = keep("ones", [P, P])
        mask_swa = keep("mask_swa", [P, 2 * P])
        mask_moba = keep("mask_moba", [P, 2 * P])
        mask_ssd = keep("mask_ssd", [P, P])
        cos2 = keep("cos2", [P, TT, HD])
        sin2 = keep("sin2", [P, TT, HD])
        cols = keep("cols", [P, DEPTH, PC_ALL])
        par = keep("par", [P, PC_ALL])
        half = keep("half", [P, PC_ROWS])
        inv_f = keep("inv_f", [P, HD // 2])
        pos_i = keep("pos_i", [P, TT], I32)
        pos_f = keep("pos_f", [P, TT])
        pool_c = keep("pool_c", [P, 4, 2])
        sq = keep("sq", [P, 2])
        ms = keep("ms", [P, 2])
        rstd = keep("rstd", [P, 2])
        neg_max = keep("neg_max", [P, 2, 2 * HEADS])
        row_max = keep("row_max", [P, 2])
        den = keep("den", [P, 2, 2 * HEADS])
        mark_pool = keep("mark_pool", [P, 16])
        mark_sb = keep("mark_sb", [P, 17])
        rden = keep("rden", [P, HEADS])
        sink_e = keep("sink_e", [P, HEADS])
        sp = keep("sp", [P, 6, TT * SSD_HEADS])
        dt_sb = keep("dt_sb", [P, TT, SSD_HEADS])
        a_dt = keep("a_dt", [P, TT, SSD_HEADS])
        acs = keep("acs", [P, TT, SSD_HEADS])
        decay = keep("decay", [P, 2, SSD_HEADS])
        ssq = keep("ssq", [P, 1])
        sms = keep("sms", [P, 1])
        srstd = keep("srstd", [P, 1])
        xmax = keep("xmax", [P, 2])
        xden = keep("xden", [P, 2])

        psum = ctx.enter_context(nc.psum_tensor("psum", [P, 8, 512], F32))

        def sem(name):
            return ctx.enter_context(nc.semaphore(name))

        raw_loaded = [Signal(sem(f"raw_loaded{i}"), 16 * len(range(i, NU, RING))) for i in range(RING)]
        mem_loaded = Signal(sem("mem_loaded"), 16)
        hi_ready = Signal(sem("hi_ready"), NU)
        lo_ready = Signal(sem("lo_ready"), NU, RING)
        unit_done = Signal(sem("unit_done"), NU, RING)
        bank_full = [sem(f"bank_full{b}") for b in range(8)]
        bank_free = [sem(f"bank_free{b}") for b in range(8)]
        par_ready = Signal(sem("par_ready"), 1)
        x_ready = Signal(sem("x_ready"), 3, 1)
        sq_done = Signal(sem("sq_done"), 8, 1)
        rstd_done = Signal(sem("rstd_done"), 4, 1)
        htok_done = Signal(sem("htok_done"), 8, 1)
        norm_hi = Signal(sem("norm_hi"), 16)
        roped = Signal(sem("roped"), 4)
        masked = Signal(sem("masked"), 16, 1)
        exp_done = Signal(sem("exp_done"), NJOBS)
        weighed = Signal(sem("weighed"), 8)
        values_done = Signal(sem("values_done"), NJOBS)
        sink_arg = Signal(sem("sink_arg"), 2)
        sink_exp = Signal(sem("sink_exp"), 2)
        conv_done = Signal(sem("conv_done"), 6)
        conv_tanh = Signal(sem("conv_tanh"), 6)
        xbc_ready = Signal(sem("xbc_ready"), 6)
        z_tanh = Signal(sem("z_tanh"), 4)
        sp_arg = Signal(sem("sp_arg"), 1)
        sp_exp = Signal(sem("sp_exp"), 1)
        adt_ready = Signal(sem("adt_ready"), 1)
        decay_arg = Signal(sem("decay_arg"), 1)
        decay_exp = Signal(sem("decay_exp"), 1)
        xdec_ready = Signal(sem("xdec_ready"), 1)
        ssd_y = Signal(sem("ssd_y"), 4)
        ssd_sq = Signal(sem("ssd_sq"), 4)
        ssd_rstd = Signal(sem("ssd_rstd"), 4, 1)
        ssd_yn = Signal(sem("ssd_yn"), 4, 1)
        close_hi = Signal(sem("close_hi"), 8)
        mg_ready = Signal(sem("mg_ready"), 4)
        mg_hi = Signal(sem("mg_hi"), 4)
        mg_lo = Signal(sem("mg_lo"), 4)
        xmax_ready = Signal(sem("xmax_ready"), 4)
        xprobs = Signal(sem("xprobs"), 4, 1)
        xo_hi = Signal(sem("xo_hi"), 4)
        relu_h = Signal(sem("relu_h"), 16)
        relu_l = Signal(sem("relu_l"), 16)
        dve_steps = sem("dve_steps")
        x_loaded, par_loaded, pos_loaded = sem("x_loaded"), sem("par_loaded"), sem("pos_loaded")
        const_made, rows_turned, cols_ready = sem("const_made"), sem("rows_turned"), sem("cols_ready")
        loga_exp, angle_ready, sines_ready = sem("loga_exp"), sem("angle_ready"), sem("sines_ready")
        gain_loaded, fin_ready, stored = sem("gain_loaded"), sem("fin_ready"), sem("stored")
        pool_steps = Signal(sem("pool_steps"), 16)
        sq_fin, ms_fin, rstd_fin = sem("sq_fin"), sem("ms_fin"), sem("rstd_fin")

        def bank(key):
            return psum[:, BANK_OF[key][0], :]

        def is_free(l, key):
            b, k = BANK_OF[key]
            return bank_free[b], l * BANK_USES[b] + (k + 1)

        def is_full(l, key):
            b, k = BANK_OF[key]
            return bank_full[b], l * FULLS[b] + (FULL_OF[key] + 1)

        def is_read(l, key):
            b, k = BANK_OF[key]
            return bank_free[b], l * BANK_USES[b] + (k + 2)

        def wait_read(eng, l, keys):
            last = {}
            for key in keys:
                b, k = BANK_OF[key]
                if b not in last or k > BANK_OF[last[b]][1]:
                    last[b] = key
            for key in last.values():
                eng.wait_ge(*is_read(l, key))

        def free(key):
            return bank_free[BANK_OF[key][0]]

        def full(key):
            return bank_full[BANK_OF[key][0]]

        FULL_OF, FULLS = {}, [0] * 8
        for key, (b, k) in sorted(BANK_OF.items(), key=lambda kv: (kv[1][0], kv[1][1])):
            if isinstance(key[0], int) or key[0] in ("down", "values"):
                continue
            FULL_OF[key] = FULLS[b]
            FULLS[b] += 1

        weights = {n: a[n] for n in ("w_in", "w_gate", "w_br_swa", "w_br_moba", "w_br_ssd", "w_mix_out",
                                     "w_cq", "w_ckv", "w_co", "w_up", "w_down")}
        inv = nc.inline_tensor(
            (np.float32(ROPE_THETA) ** (-np.arange(HD // 2, dtype=np.float32) / np.float32(HD // 2)))
            .astype(np.float32)[None, :], "rope_inverse_frequencies")
        block = ctx.enter_context(nc.Block())

        def prev_user(u):
            return u - RING if u >= RING else max(v for v in range(NU) if v % RING == u % RING) - NU

        def unit_bank(u, i):
            return unit_banks(u, UNITS[u])[i]

        def wide(ap, n):
            return ap.unsqueeze(2).to_broadcast([P, ap.shape[1], n])

        @block.sync
        def _(sp):
            sp.dma_start(x_sb[:], a["x"].rearrange("b (t p) d -> p (b t) d", p=P)).then_inc(x_loaded, 16)
            lay = "l (k p) -> k l p"
            for name, r0, n in (("norm_mix", 0, 8), ("norm_cross", 8, 8), ("norm_mem", 16, 8),
                                ("norm_mlp", 24, 8), ("ssd_norm", PC_SSDN, 8), ("conv_b", PC_CONVB, 12),
                                ("b_gate", PC_BGATE, 24)):
                sp.dma_start(rows[r0:r0 + n, :, :], a[name].rearrange(lay, p=P)).then_inc(par_loaded, 16)
            for l in range(DEPTH):
                sp.dma_start(rows[PC_CONVW:PC_CONVB, l, :],
                             a["conv_w"][l].rearrange("t (c p) -> (t c) p", p=P)).then_inc(par_loaded, 16)
            for name, c0, n in (("dt_bias", PC_DTB, SSD_HEADS), ("a_log", PC_NEGA, SSD_HEADS),
                                ("d_skip", PC_DSKIP, SSD_HEADS), ("swa_sinks", PC_SINK, HEADS)):
                sp.dma_start(cols[:, :, c0:c0 + n], a[name].partition_broadcast(P)).then_inc(par_loaded, 16)
            sp.dma_start(pos_i[:], a["positions"].rearrange("b (t p) -> p (b t)", p=P),
                         allow_slow_non_contiguous=True).then_inc(pos_loaded, 16)
            sp.dma_start(inv_f[:], inv.ap()[0].partition_broadcast(P)).then_inc(pos_loaded, 16)

            with sp.Fori(0, DEPTH) as l:
                for u, w in enumerate(UNITS):
                    if u == U_MIX - 2:
                        sp.wait_ge(*ssd_y.at(l, 4))
                        sp.dma_start(mem_sb[:], a["mem"].rearrange("b (t p) d -> p (b t) d", p=P))\
                          .then_inc(mem_loaded.sem, 16)
                    n = w["kt"] * w["cols"]
                    sp.wait_ge(*lo_ready.at(l, prev_user(u) + 1))
                    src = weights[w["weight"]][l, w["row"]:w["row"] + w["kt"] * P, w["col"]:w["col"] + w["cols"]]
                    sp.dma_start(raw[:, u % RING, 0:n].rearrange("p (k n) -> p k n", n=w["cols"]),
                                 src.rearrange("(k p) n -> p k n", p=P)).then_inc(raw_loaded[u % RING].sem, 16)

            sp.wait_ge(*unit_done.at(DEPTH, 0))
            sp.dma_start(gain[:], a["final_norm"].partition_broadcast(P)).then_inc(gain_loaded, 16)
            sp.wait_ge(fin_ready, TT)
            sp.dma_start(out.rearrange("b (t p) d -> p (b t) d", p=P), h_tok[:]).then_inc(stored, 16)
            sp.wait_ge(stored, 16)

        @block.gpsimd
        def _(pool):
            pool.memset(pool_c[:, 0, :], 1.0 / D).then_inc(lo_ready.sem, RING)
            pool.memset(ident[:], 0.0).then_inc(unit_done.sem, RING)
            credited = [sig.sem for sig in (x_ready, rstd_done, sq_done, htok_done, ssd_rstd, ssd_yn, xprobs, masked)]
            for i, s in enumerate(credited + bank_free):
                pool.memset(mark_pool[:, i:i + 1], 0.0).then_inc(s, 1)
            for i, value in ((1, SSD_GROUPS / D), (2, EPS), (3, -0.5)):
                pool.memset(pool_c[:, i, :], value).then_inc(const_made, 1)
            for i, (tile, value) in enumerate(((tri, 1.0), (ones, 1.0), (mask_swa, 0.0), (mask_moba, 0.0),
                                               (mask_ssd, 0.0))):
                pool.memset(tile[:], value).then_inc(const_made, 1)
            pool.wait_ge(const_made, 8)
            pool.wait_ge(lo_ready.sem, RING)
            pool.wait_ge(unit_done.sem, RING)

            def select(ap, step, base, channel, op, fill):
                pool.affine_select(out=ap, in_=ap, pattern=[[step, P]], compare_op=op, fill=fill, base=base,
                                   channel_multiplier=channel).then_inc(const_made, 1)

            select(ident[:], 1, 0, -1, ALU.not_equal, 1.0)
            select(tri[:], 1, 0, -1, ALU.is_ge, 0.0)
            select(mask_ssd[:], 1, 0, -1, ALU.is_ge, NEG)
            select(mask_swa[:, 0:P], 1, 0, -1, ALU.is_gt, NEG)
            select(mask_swa[:, P:2 * P], -1, 0, 1, ALU.is_ge, NEG)
            select(mask_moba[:, P:2 * P], -1, 0, 1, ALU.is_ge, NEG)

            def step(sem, value, ins):
                ins.then_inc(sem, 1)
                pool.wait_ge(sem, value)

            def norm(l, n):
                before = 2 * n + (8 if n else 0)
                pool.wait_ge(*sq_done.at(l, 2 * n + 2))
                step(*pool_steps.at(l, before + 1), pool.tensor_tensor(ms[:], sq[:], pool_c[:, 0, :], ALU.mult))
                step(*pool_steps.at(l, before + 2), pool.tensor_tensor(ms[:], ms[:], pool_c[:, 2, :], ALU.add))
                pool.wait_ge(*htok_done.at(l, 2 * n))
                pool.tensor_tensor(rstd[:], ms[:], pool_c[:, 3, :], ALU.pow).then_inc(rstd_done.sem, 1)

            with pool.Fori(0, DEPTH) as l:
                norm(l, 0)
                for c in range(4):
                    before = 2 + 2 * c
                    pool.wait_ge(*ssd_sq.at(l, c + 1))
                    step(*pool_steps.at(l, before + 1), pool.tensor_tensor(sms[:], ssq[:], pool_c[:, 1, 0:1], ALU.mult))
                    step(*pool_steps.at(l, before + 2), pool.tensor_tensor(sms[:], sms[:], pool_c[:, 2, 0:1], ALU.add))
                    pool.wait_ge(*ssd_yn.at(l, c))
                    pool.tensor_tensor(srstd[:], sms[:], pool_c[:, 3, 0:1], ALU.pow).then_inc(ssd_rstd.sem, 1)
                for n in (1, 2, 3):
                    norm(l, n)
            pool.wait_ge(sq_fin, 2)
            step(ms_fin, 1, pool.tensor_tensor(ms[:], sq[:], pool_c[:, 0, :], ALU.mult))
            step(ms_fin, 2, pool.tensor_tensor(ms[:], ms[:], pool_c[:, 2, :], ALU.add))
            pool.wait_ge(*htok_done.at(DEPTH, 0))
            pool.tensor_tensor(rstd[:], ms[:], pool_c[:, 3, :], ALU.pow).then_inc(rstd_fin, 1)

        NCONST = 14
        NPAR = 16 * (7 + DEPTH + 4)

        @block.scalar
        def _(act):
            act.wait_ge(par_loaded, NPAR)
            act.activation(cols[:, :, PC_NEGA:PC_DSKIP], cols[:, :, PC_NEGA:PC_DSKIP], ACT.Exp)\
               .then_inc(loga_exp, 1)
            act.wait_ge(angle_ready, 1)
            act.activation(cos2[:, :, 0:32], cos2[:, :, 0:32], ACT.Sin).then_inc(sines_ready, 1)
            act.activation(sin2[:, :, 32:64], sin2[:, :, 32:64], ACT.Sin).then_inc(sines_ready, 1)

            def hi(l, u):
                w, slot = UNITS[u], u % RING
                n = w["kt"] * w["cols"]
                act.wait_ge(*raw_loaded[slot].at(l, 16 * (u // RING + 1)))
                act.wait_ge(*unit_done.at(l, prev_user(u) + 1))
                act.activation(w_hi[:, slot, 0:n], raw[:, slot, 0:n], ACT.Copy).then_inc(hi_ready.sem, 1)

            def norm_square(l, n):
                if n == 1:
                    act.wait_ge(*mem_loaded.at(l, 16))
                    act.wait_ge(*mg_ready.at(l, 4))
                else:
                    act.wait_ge(*x_ready.at(l, {0: 0, 2: 1, 3: 2}[n]))
                act.wait_ge(*rstd_done.at(l, n))
                act.wait_ge(*sq_done.at(l, 2 * n))
                src = mem_sb if n == 1 else x_sb
                for t in range(TT):
                    act.activation(tmp[:, t, :].bitcast(mybir.dt.bfloat16), src[:, t, :], ACT.Square,
                                   accum_out=sq[:, t:t + 1]).then_inc(sq_done.sem, 1)

            def norm_gain_hi(l, n):
                dst = hm_hi if n == 1 else act_hi
                if n == 1:
                    act.wait_ge(*unit_done.at(l, U_MIX))
                if n == 2:
                    act.wait_ge(*unit_done.at(l, U_KX))
                for b in range(4):
                    act.wait_ge(*is_full(l, ("norm", n, b)))
                    for kk in range(2):
                        k = 2 * b + kk
                        ins = act.activation(dst[:, k, :], bank(("norm", n, b))[:, kk * SEQ:(kk + 1) * SEQ],
                                             ACT.Copy, scale=par[:, PC_NORM[n] + k:PC_NORM[n] + k + 1])
                    ins.then_inc(norm_hi.sem, 1)

            def out_of_bank(l, key, dst, src=None):
                src = bank(key) if src is None else src
                act.activation(dst, src, ACT.Copy).then_inc(free(key), 1)

            def two(ap):
                return ap.rearrange("p (k n) -> p k n", n=SEQ)

            def evacuate(l, u):
                w, j = UNITS[u], UNITS[u]["index"]
                kind = w["kind"]
                if not w["last"] or kind in ("qa", "kva", "dt", "branch_a", "branch_b", "branch_c", "mix",
                                             "co", "down"):
                    return
                if kind == "xbc":
                    act.wait_ge(*conv_done.at(l, j + 1))
                    act.activation(tmp[:, 1, :], tmp[:, 0, :], ACT.Tanh).then_inc(conv_tanh.sem, 1)
                    return
                if kind == "up":
                    act.wait_ge(*unit_done.at(l, u + 1))
                    if j >= 2:
                        act.wait_ge(*relu_l.at(l, j - 1))
                    act.activation(tmp[:, j % 2, :], bank((u, 0)), ACT.Relu).then_inc(free((u, 0)), 1)
                    act.wait_ge(*is_read(l, (u, 0)))
                    act.activation(relu_hi[:, (j // 2) % 2, 2 * (j % 2):2 * (j % 2) + 2, :], two(tmp[:, j % 2, :]),
                                   ACT.Square).then_inc(relu_h.sem, 1)
                    return
                act.wait_ge(*unit_done.at(l, u + 1))
                if kind == "qkb":
                    out_of_bank(l, (u, 0), qkT_b[:, 2 * j:2 * j + 2, :], two(bank((u, 0))))
                elif kind == "kx":
                    out_of_bank(l, (u, 0), k_xT[:, 2 * j:2 * j + 2, :], two(bank((u, 0))))
                elif kind == "qx":
                    out_of_bank(l, (u, 0), q_xT[:, 2 * j:2 * j + 2, :], two(bank((u, 0))))
                elif kind in ("vb", "vx"):
                    for t in range(TT):
                        key = unit_bank(u, t)
                        dst = v_b[:, t, :] if kind == "vb" else v_x[:, t, 512 * j:512 * j + 512]
                        out_of_bank(l, key, dst)
                elif kind == "z":
                    if j == 0:
                        act.wait_ge(*xbc_ready.at(l, 6))
                    for t in range(TT):
                        if j == 1:
                            act.wait_ge(*is_read(l, unit_bank(U_Z + 1, t)))
                        act.activation(tmp[:, t, :], bank(unit_bank(u, t)), ACT.Tanh, scale=0.5)\
                           .then_inc(z_tanh.sem, 1)
                elif kind == "gate":
                    branch, tile = w["col"] // D, (w["col"] % D) // P
                    if branch == 1:
                        act.wait_ge(*is_read(l, (U_BRA + 1, 1)))
                    if branch == 2:
                        act.wait_ge(*is_read(l, (U_BRB + 1, 1)))
                    for m in range(2):
                        b0 = PC_BGATE + branch * KT + tile + m
                        ins = act.activation(g_sb[:, tile + m, :], bank((u, 0))[:, m * SEQ:(m + 1) * SEQ],
                                             ACT.Tanh, bias=half[:, b0:b0 + 1], scale=0.5)
                    ins.then_inc(free((u, 0)), 1)

            def merged_hi(l, j):
                act.wait_ge(*mg_ready.at(l, j + 1))
                act.activation(act_hi[:, 2 * j:2 * j + 2, :], mg_sb[:, 2 * j:2 * j + 2, :], ACT.Copy, scale=0.5)\
                   .then_inc(mg_hi.sem, 1)

            def turned_probs(l, n):
                if not 0 <= n < 16:
                    return
                n_cols = 2 * (job_of(n)[1] + 1) * P
                act.wait_ge(*is_full(l, ("probsT", n)))
                if n >= 2:
                    act.wait_ge(*values_done.at(l, n - 1))
                out_of_bank(l, ("probsT", n), pT_sb[:, n % 2, 0:n_cols], bank(("probsT", n))[:, 0:n_cols])

            def exps(l, n):
                if not 0 <= n < NJOBS:
                    return
                branch, t, j = job_of(n)
                if branch == 2:
                    act.wait_ge(*is_read(l, ("score", n)))
                    act.activation(s_sb[:, n % 2, :], s_sb[:, n % 2, :], ACT.Exp).then_inc(exp_done.sem, 1)
                    return
                act.wait_ge(*masked.at(l, n + 1))
                keys = (t + 1) * P
                for i in range(2):
                    h = HEADS * t + head_of(j, i)
                    s = s_sb[:, n % 2, i * 2 * P:i * 2 * P + keys]
                    ins = act.activation(s, s, ACT.Exp, bias=neg_max[:, branch, h:h + 1], scale=ATT_SCALE,
                                         accum_out=den[:, branch, h:h + 1])
                ins.then_inc(exp_done.sem, 1)
                if branch == 0 and j == 3:
                    act.wait_ge(*sink_arg.at(l, t + 1))
                    act.activation(sink_e[:], sink_e[:], ACT.Exp).then_inc(sink_exp.sem, 1)

            def close_scale(l, i):
                act.wait_ge(*ssd_rstd.at(l, i - 3))
                act.activation(y_tok[:], y_tok[:], ACT.Copy, scale=srstd[:]).then_inc(ssd_yn.sem, 1)

            def close_square(l, i):
                act.wait_ge(*ssd_y.at(l, i - 3))
                act.wait_ge(*ssd_rstd.at(l, i - 4))
                if i > 4:
                    act.wait_ge(*ssd_sq.at(l, i - 4))
                act.activation(xdec[:, 0:512], y_tok[:], ACT.Square, accum_out=ssq[:]).then_inc(ssd_sq.sem, 1)

            def close_hi_part(l, i):
                _, branch, t, g = CLOSINGS[i]
                src = bank(("closeT", i))
                act.wait_ge(*is_full(l, ("closeT", i)))
                if branch < 2:
                    dst = (ya_hi, yb_hi)[branch]
                    act.activation(dst[:, :, t * P:(t + 1) * P], src.rearrange("p (k n) -> p k n", n=P), ACT.Copy)\
                       .then_inc(close_hi.sem, 1)
                    return
                if i == 4:
                    act.wait_ge(*values_done.at(l, 16))
                for k in range(4):
                    c = PC_SSDN + 4 * g + k
                    ins = act.activation(yc_hi[:, 4 * g + k, t * P:(t + 1) * P], src[:, k * P:(k + 1) * P], ACT.Copy,
                                         scale=par[:, c:c + 1])
                ins.then_inc(close_hi.sem, 1)

            def cross_exps(l, h):
                act.wait_ge(*xmax_ready.at(l, h + 1))
                if h >= 2:
                    act.wait_ge(*is_full(l, ("xprobsT", h - 2)))
                act.wait_ge(*xprobs.at(l, h))
                for t in range(TT):
                    ins = act.activation(s_sb[:, h % 2, t * SEQ:(t + 1) * SEQ],
                                         bank(("xscore", h))[:, t * SEQ:(t + 1) * SEQ], ACT.Exp,
                                         bias=xmax[:, t:t + 1], scale=X_SCALE, accum_out=xden[:, t:t + 1])
                ins.then_inc(free(("xscore", h)), 1)

            def cross_out_hi(l, h):
                act.wait_ge(*is_full(l, ("xvalues", h)))
                act.activation(o_hi[:, 2 * h:2 * h + 2, :], two(bank(("xvalues", h))), ACT.Copy)\
                   .then_inc(xo_hi.sem, 1)

            act.wait_ge(x_loaded, 16)
            with act.Fori(0, DEPTH) as l:
                norm_square(l, 0)
                act.wait_ge(*par_ready.at(l, 1))
                hi(l, 0)
                norm_gain_hi(l, 0)
                hi(l, 1)
                hi(l, 2)
                for u, w in enumerate(UNITS):
                    n, h = u - JOB_SLOT0, u - CROSS_SLOT0
                    for i in range(4, 8):
                        if u == CLOSE_SLOT[i] + 1:
                            close_scale(l, i)
                    if u == SWA_T_SLOT:
                        for i in range(3):
                            act.wait_ge(*is_full(l, ("qkT", i)))
                            out_of_bank(l, ("qkT", i), qkT_a[:, 2 * i:2 * i + 2, :], two(bank(("qkT", i))))
                    turned_probs(l, n - 1)
                    for i in range(8):
                        if u == CLOSE_SLOT[i] + 1:
                            close_hi_part(l, i)
                    if u == CB_SLOT:
                        act.wait_ge(*is_full(l, ("cb",)))
                        out_of_bank(l, ("cb",), cbT[:].rearrange("p k n -> p (k n)"))
                    if u == BTOK_SLOT:
                        act.wait_ge(*is_full(l, ("btok",)))
                        out_of_bank(l, ("btok",), b_tok[:].rearrange("p k n -> p (k n)"), bank(("btok",))[:, 0:SEQ])
                    if u == STATES_SLOT:
                        for g in range(SSD_GROUPS):
                            act.wait_ge(*is_full(l, ("states", g)))
                            out_of_bank(l, ("states", g), states[:, g, :])
                    if 0 <= h - 1 < X_HEADS:
                        act.wait_ge(*is_full(l, ("xprobsT", h - 1)))
                        out_of_bank(l, ("xprobsT", h - 1), pT_x[:, h - 1, :, :], two(bank(("xprobsT", h - 1))))
                    evacuate(l, u)
                    if w["kind"] == "branch_c":
                        merged_hi(l, w["index"])
                    if u + RING < NU:
                        hi(l, u + RING)
                    if u == ACS_SLOT - 1:
                        act.wait_ge(*sp_arg.at(l, 1))
                        act.activation(sp[:, 1, :], sp[:, 0, :], ACT.Exp, scale=-1.0).then_inc(sp_exp.sem, 1)
                    if u == ACS_SLOT:
                        act.wait_ge(*decay_arg.at(l, 1))
                        act.activation(decay[:], decay[:], ACT.Exp).then_inc(decay_exp.sem, 1)
                    for i in range(4, 8):
                        if u == CLOSE_SLOT[i]:
                            close_square(l, i)
                    exps(l, n)
                    if 0 <= h < X_HEADS:
                        cross_exps(l, h)
                    for hh in {U_VX + 2: (0, 1), U_VX + 3: (2, 3)}.get(u, ()):
                        cross_out_hi(l, hh)
                    for n in (1, 2, 3):
                        if u == NORM_SCALE_SLOT[n]:
                            norm_square(l, n)
                        if u == NORM_TURN_SLOT[n]:
                            norm_gain_hi(l, n)
            act.wait_ge(*x_ready.at(DEPTH, 0))
            act.wait_ge(*rstd_done.at(DEPTH, 0))
            act.wait_ge(*sq_done.at(DEPTH, 0))
            for t in range(TT):
                act.activation(tmp[:, t, :].bitcast(mybir.dt.bfloat16), x_sb[:, t, :], ACT.Square,
                               accum_out=sq[:, t:t + 1]).then_inc(sq_fin, 1)

        @block.tensor
        def _(pe):
            pe.wait_ge(const_made, NCONST)
            pe.wait_ge(par_loaded, NPAR)
            for l in range(DEPTH):
                pe.transpose(psum[:, l, 0:PC_ROWS], rows[0:PC_ROWS, l, :], ident[0:PC_ROWS, 0:PC_ROWS])\
                  .then_inc(rows_turned, 1)
            pe.wait_ge(cols_ready, 1)

            operands = {"h": (act_hi, act_lo), "merged": (act_hi, act_lo), "hq": (act_hi, act_lo),
                        "hf": (act_hi, act_lo), "mem": (hm_hi, hm_lo), "o": (o_hi, o_lo),
                        "y_swa": (ya_hi, ya_lo), "y_moba": (yb_hi, yb_lo), "y_ssd": (yc_hi, yc_lo)}

            def operand_ready(l, u):
                w = UNITS[u]
                act, j = w["act"], w["index"]
                if act == "relu":
                    pe.wait_ge(*relu_l.at(l, 2 * (j // 2) + 2))
                elif act == "merged":
                    pe.wait_ge(*mg_lo.at(l, 2 if w["first"] else 4))
                elif u > 0 and UNITS[u - 1]["act"] == act:
                    return
                elif act in ("h", "mem", "hq", "hf"):
                    for b in range(4):
                        pe.wait_ge(*is_read(l, ("norm", {"h": 0, "mem": 1, "hq": 2, "hf": 3}[act], b)))
                elif act == "o":
                    wait_read(pe, l, [("xvalues", h) for h in range(X_HEADS)])
                else:
                    pe.wait_ge(*is_read(l, ("closeT", {"y_swa": 1, "y_moba": 3, "y_ssd": 7}[act])))

            def unit(l, u):
                w, slot = UNITS[u], u % RING
                kt, n = w["kt"], w["cols"]
                pe.wait_ge(*lo_ready.at(l, u + 1))
                operand_ready(l, u)
                if w["first"]:
                    for key in unit_banks(u, w):
                        pe.wait_ge(*is_free(l, key))
                if w["act"] == "relu":
                    a_hi, a_lo = relu_hi[:, (w["index"] // 2) % 2], relu_lo[:, (w["index"] // 2) % 2]
                else:
                    a_hi, a_lo = operands[w["act"]][0][:], operands[w["act"]][1][:]
                m_hi = w_hi[:, slot, 0:kt * n].rearrange("p (k n) -> p k n", n=n)
                m_lo = w_lo[:, slot, 0:kt * n].rearrange("p (k n) -> p k n", n=n)
                k0 = w["row"] // P if w["act"] != "relu" else 0
                if w["orient"] == "A":
                    for m in range(n // P):
                        dst = bank(unit_banks(u, w)[m // 2])[:, (m % 2) * SEQ:(m % 2 + 1) * SEQ]
                        for k in range(kt):
                            cs = slice(m * P, (m + 1) * P)
                            pe.matmul(dst, m_hi[:, k, cs], a_hi[:, k, :], start=k == 0, stop=False)
                            pe.matmul(dst, m_hi[:, k, cs], a_lo[:, k, :], start=False, stop=False)
                            ins = pe.matmul(dst, m_lo[:, k, cs], a_hi[:, k, :], start=False, stop=k == kt - 1)
                else:
                    for t in range(TT):
                        keys = unit_banks(u, w)
                        dst = bank(keys[t])[:, 0:n] if len(keys) == TT else bank(keys[0])[:, t * n:(t + 1) * n]
                        for k in range(kt):
                            first, last = w["first"] and k == 0, w["last"] and k == kt - 1
                            ts = slice(t * P, (t + 1) * P)
                            pe.matmul(dst, a_hi[:, k0 + k, ts], m_hi[:, k, :], start=first, stop=False)
                            pe.matmul(dst, a_hi[:, k0 + k, ts], m_lo[:, k, :], start=False, stop=False)
                            ins = pe.matmul(dst, a_lo[:, k0 + k, ts], m_hi[:, k, :], start=False, stop=last)
                ins.then_inc(unit_done.sem, 1)

            def norm_turn(l, n):
                for t in range(TT):
                    pe.wait_ge(*htok_done.at(l, 2 * n + t + 1))
                for b in range(4):
                    key = ("norm", n, b)
                    pe.wait_ge(*is_free(l, key))
                    for kk in range(2):
                        for t in range(TT):
                            k = 2 * b + kk
                            ins = pe.transpose(bank(key)[:, kk * SEQ + t * P:kk * SEQ + (t + 1) * P],
                                               h_tok[:, t, k * P:(k + 1) * P], ident[:])
                    ins.then_inc(full(key), 1)

            def swa_turn(l):
                pe.wait_ge(*roped.at(l, 4))
                for i in range(3):
                    key = ("qkT", i)
                    pe.wait_ge(*is_free(l, key))
                    for kk in range(2):
                        for t in range(TT):
                            k = 2 * i + kk
                            ins = pe.transpose(bank(key)[:, kk * SEQ + t * P:kk * SEQ + (t + 1) * P],
                                               qk_tok[:, t, k * P:(k + 1) * P], ident[:])
                    ins.then_inc(full(key), 1)

            def job_scores(l, n):
                branch, t, j = job_of(n)
                key = ("score", n)
                if n == 0:
                    wait_read(pe, l, [("qkT", i) for i in range(1, 3)])
                if n == 8:
                    wait_read(pe, l, [(U_QKB + i, 0) for i in range(4)] + [unit_bank(U_VB, t) for t in range(TT)])
                if n == 16:
                    pe.wait_ge(*adt_ready.at(l, 1))
                pe.wait_ge(*is_free(l, key))
                if branch == 2:
                    for i in range(4):
                        ins = pe.matmul(bank(key)[:, i * P:(i + 1) * P],
                                        a_dt[:, t, 4 * j + i:4 * j + i + 1].to_broadcast([P, P]), tri[:],
                                        start=True, stop=True)
                else:
                    qk = (qkT_a, qkT_b)[branch]
                    half_p = slice((j % 2) * HD, (j % 2 + 1) * HD)
                    for i in range(2):
                        q_tile = head_of(j, i) // 2
                        k_tile = 4 + (j // 2 if branch == 0 else q_tile)
                        ins = pe.matmul(bank(key)[:, i * 2 * P:i * 2 * P + (t + 1) * P],
                                        qk[half_p, q_tile, t * P:(t + 1) * P], qk[half_p, k_tile, 0:(t + 1) * P],
                                        start=True, stop=True)
                ins.then_inc(full(key), 1)

            def job_turn(l, n):
                branch, t, j = job_of(n)
                if branch == 2:
                    return
                key = ("probsT", n)
                pe.wait_ge(*exp_done.at(l, n + 1))
                pe.wait_ge(*is_free(l, key))
                for i in range(2):
                    for k in range(t + 1):
                        c = (i * (t + 1) + k) * P
                        ins = pe.transpose(bank(key)[:, c:c + P], s_sb[:, n % 2, i * 2 * P + k * P:i * 2 * P + (k + 1) * P],
                                           ident[:])
                ins.then_inc(full(key), 1)

            def job_values(l, n):
                branch, t, j = job_of(n)
                if branch < 2:
                    opens = n - j
                    pe.wait_ge(*is_read(l, ("probsT", n)))
                else:
                    opens = n - j % 2
                    pe.wait_ge(*weighed.at(l, n - 15))
                    if n == 16:
                        wait_read(pe, l, [("xs", 1, 0), ("xs", 1, 1)])
                key = ("values", opens)
                if n == opens:
                    pe.wait_ge(*is_free(l, key))
                if branch == 2:
                    for i in range(4):
                        c = (4 * (j % 2) + i) * HD
                        ins = pe.matmul(bank(key)[:, c:c + HD], s_sb[:, n % 2, i * P:(i + 1) * P],
                                        xdt[:, t, (4 * j + i) * HD:(4 * j + i + 1) * HD], start=True, stop=True)
                else:
                    for i in range(2):
                        hs = slice(head_of(j, i) * HD, (head_of(j, i) + 1) * HD)
                        for k in range(t + 1):
                            v = v_a[:, k, (j // 2) * HD:(j // 2 + 1) * HD] if branch == 0 else v_b[:, k, hs]
                            c = (i * (t + 1) + k) * P
                            ins = pe.matmul(bank(key)[:, hs],
                                            pT_sb[:, n % 2, c:c + P], v, start=k == 0, stop=k == t)
                ins.then_inc(values_done.sem, 1)

            def close_turn(l, i):
                job, branch = CLOSINGS[i][:2]
                key = ("closeT", i)
                if branch < 2:
                    pe.wait_ge(*is_read(l, ("values", job - 3)))
                else:
                    pe.wait_ge(*ssd_yn.at(l, i - 3))
                pe.wait_ge(*is_free(l, key))
                for k in range(4):
                    ins = pe.transpose(bank(key)[:, k * P:(k + 1) * P], y_tok[:, k * P:(k + 1) * P], ident[:])
                ins.then_inc(full(key), 1)

            def cross_scores(l, h):
                key = ("xscore", h)
                wait_read(pe, l, ([(U_KX + i, 0) for i in range(4)] if h == 0 else []) + [(U_QX + h, 0)])
                pe.wait_ge(*is_free(l, key))
                for t in range(TT):
                    for kk in range(2):
                        ins = pe.matmul(bank(key)[:, t * SEQ:(t + 1) * SEQ], q_xT[:, 2 * h + kk, t * P:(t + 1) * P],
                                        k_xT[:, 2 * h + kk, :], start=kk == 0, stop=kk == 1)
                ins.then_inc(full(key), 1)

            def cross_turn(l, h):
                key = ("xprobsT", h)
                pe.wait_ge(*xprobs.at(l, h + 1))
                pe.wait_ge(*is_free(l, key))
                for t in range(TT):
                    for m in range(2):
                        ins = pe.transpose(bank(key)[:, m * SEQ + t * P:m * SEQ + (t + 1) * P],
                                           s_sb[:, h % 2, t * SEQ + m * P:t * SEQ + (m + 1) * P], ident[:])
                ins.then_inc(full(key), 1)

            def cross_values(l, h):
                key = ("xvalues", h)
                for t in range(TT):
                    pe.wait_ge(*is_read(l, unit_bank(U_VX + 1 + 2 * (h // 2), t)))
                pe.wait_ge(*is_read(l, ("xprobsT", h)))
                pe.wait_ge(*is_free(l, key))
                for dd in range(2):
                    for m in range(2):
                        c = h * SEQ + dd * P
                        ins = pe.matmul(bank(key)[:, dd * SEQ:(dd + 1) * SEQ], v_x[:, m, c:c + P], pT_x[:, h, m, :],
                                        start=m == 0, stop=m == 1)
                ins.then_inc(full(key), 1)

            with pe.Fori(0, DEPTH) as l:
                norm_turn(l, 0)
                for u in range(NU):
                    unit(l, u)
                    n, h = u - JOB_SLOT0, u - CROSS_SLOT0
                    if u == SWA_T_SLOT:
                        swa_turn(l)
                    if 0 <= n < NJOBS:
                        job_scores(l, n)
                    if 0 <= n - 1 < NJOBS:
                        job_turn(l, n - 1)
                    if 0 <= n - 2 < NJOBS:
                        job_values(l, n - 2)
                    if u == ACS_SLOT:
                        pe.wait_ge(*adt_ready.at(l, 1))
                        pe.wait_ge(*is_free(l, ("acs",)))
                        dst = bank(("acs",))
                        pe.matmul(dst[:, 0:2 * SSD_HEADS], tri[:], a_dt[:].rearrange("p t h -> p (t h)"),
                                  start=True, stop=True)
                        pe.matmul(dst[:, 2 * SSD_HEADS:3 * SSD_HEADS], ones[:], a_dt[:, 0, :],
                                  start=True, stop=True).then_inc(full(("acs",)), 1)
                    if u == CB_SLOT:
                        pe.wait_ge(*xbc_ready.at(l, 6))
                        pe.wait_ge(*is_free(l, ("cb",)))
                        for c in range(TT):
                            for g in range(SSD_GROUPS):
                                i = SSD_GROUPS * c + g
                                ins = pe.matmul(bank(("cb",))[:, i * P:(i + 1) * P], xbcT[:, 8 + g, c * P:(c + 1) * P],
                                                xbcT[:, 10 + g, c * P:(c + 1) * P], start=True, stop=True)
                        ins.then_inc(full(("cb",)), 1)
                    if u == BTOK_SLOT:
                        pe.wait_ge(*is_free(l, ("btok",)))
                        for g in range(SSD_GROUPS):
                            ins = pe.transpose(bank(("btok",))[:, g * P:(g + 1) * P], xbcT[:, 8 + g, 0:P], ident[:])
                        ins.then_inc(full(("btok",)), 1)
                    if u in (XS_SLOT, XS_SLOT + 1):
                        g = u - XS_SLOT
                        for t in range(TT):
                            key = ("xs", g, t)
                            pe.wait_ge(*is_free(l, key))
                            for k in range(4):
                                ins = pe.transpose(bank(key)[:, k * P:(k + 1) * P],
                                                   xbcT[:, 4 * g + k, t * P:(t + 1) * P], ident[:])
                            ins.then_inc(full(key), 1)
                    if u == STATES_SLOT:
                        pe.wait_ge(*xdec_ready.at(l, 1))
                        for g in range(SSD_GROUPS):
                            key = ("states", g)
                            pe.wait_ge(*is_free(l, key))
                            pe.matmul(bank(key), b_tok[:, g, :], xdec[:, 512 * g:512 * (g + 1)],
                                      start=True, stop=True).then_inc(full(key), 1)
                    for i in range(8):
                        if u == CLOSE_SLOT[i] + 1:
                            close_turn(l, i)
                    for i, (_, branch, c, g) in enumerate(CLOSINGS):
                        if branch == 2 and c == 1 and u == CLOSE_SLOT[i]:
                            key = ("yoff", g)
                            if g == 1:
                                pe.wait_ge(*is_read(l, ("states", 1)))
                            pe.wait_ge(*is_free(l, key))
                            pe.matmul(bank(key), xbcT[:, 10 + g, P:2 * P], states[:, g, :],
                                      start=True, stop=True).then_inc(full(key), 1)
                    if 0 <= h < X_HEADS:
                        cross_scores(l, h)
                    if 0 <= h - 1 < X_HEADS:
                        cross_turn(l, h - 1)
                    for hh in {U_VX + 2: (0, 1), U_VX + 3: (2, 3)}.get(u, ()):
                        cross_values(l, hh)
                    for n in (1, 2, 3):
                        if u == NORM_TURN_SLOT[n]:
                            norm_turn(l, n)

        @block.vector
        def _(dve):
            steps = Steps(dve, dve_steps, DVE_STEPS)
            TWO_PI = 2.0 * math.pi
            PI_PARTS = (6.28125, 0.0019350051879882812, TWO_PI - 6.28125 - 0.0019350051879882812)
            ROUND = 1.5 * 2.0 ** 23

            dve.wait_ge(rows_turned, DEPTH)
            for l in range(DEPTH):
                steps.mark(dve.tensor_copy(cols[:, l, 0:PC_ROWS], psum[:, l, 0:PC_ROWS]))
            dve.wait_ge(loga_exp, 1)
            steps.mark(dve.tensor_scalar(cols[:, :, PC_NEGA:PC_DSKIP], cols[:, :, PC_NEGA:PC_DSKIP], -1.0, None,
                                         ALU.mult))
            dve.tensor_scalar(cols[:, :, PC_SINK:PC_ALL], cols[:, :, PC_SINK:PC_ALL], 1.0 / ATT_SCALE, None,
                              ALU.mult).then_inc(cols_ready, 1)
            steps.settle()
            dve.wait_ge(cols_ready, 1)

            dve.wait_ge(pos_loaded, 32)
            steps.link(dve.tensor_copy(pos_f[:], pos_i[:]))
            turns = tmp[:, 0, 0:64].rearrange("p (t n) -> p t n", n=32)
            angle = tmp[:, 0, 64:128].rearrange("p (t n) -> p t n", n=32)
            for t in range(TT):
                steps.mark(dve.tensor_scalar(angle[:, t, :], inv_f[:], pos_f[:, t:t + 1], None, ALU.mult))
            steps.settle()
            for shift, dst in ((0.25, cos2[:, :, 0:32]), (0.0, sin2[:, :, 32:64])):
                steps.link(dve.tensor_scalar(turns, angle, 1.0 / TWO_PI, shift, ALU.mult, ALU.add))
                steps.link(dve.tensor_scalar(turns, turns, ROUND, None, ALU.add))
                steps.link(dve.tensor_scalar(turns, turns, ROUND, None, ALU.subtract))
                src = angle
                for part in PI_PARTS:
                    steps.link(dve.scalar_tensor_tensor(dst, turns, -part, src, ALU.mult, ALU.add))
                    src = dst
                steps.link(dve.tensor_scalar(dst, dst, shift * TWO_PI, 3.1415925, ALU.add, ALU.min))
                ins = dve.tensor_scalar(dst, dst, -3.1415925, None, ALU.max)
                if shift:
                    steps.link(ins)
                else:
                    ins.then_inc(angle_ready, 1)
            dve.wait_ge(sines_ready, 2)
            steps.mark(dve.tensor_copy(cos2[:, :, 32:64], cos2[:, :, 0:32]))
            steps.mark(dve.tensor_scalar(sin2[:, :, 0:32], sin2[:, :, 32:64], -1.0, None, ALU.mult))
            steps.settle()
            dve.wait_ge(x_loaded, 16)
            dve.wait_ge(const_made, NCONST)

            def lo(l, u):
                slot, n = u % RING, UNITS[u]["kt"] * UNITS[u]["cols"]
                dve.wait_ge(*hi_ready.at(l, u + 1))
                dve.tensor_tensor(w_lo[:, slot, 0:n], raw[:, slot, 0:n], w_hi[:, slot, 0:n].bitcast(F32),
                                  ALU.subtract).then_inc(lo_ready.sem, 1)

            def two(ap):
                return ap.rearrange("p (k n) -> p k n", n=SEQ)

            def norm_scale(l, n):
                dve.wait_ge(*rstd_done.at(l, n + 1))
                src = mem_sb if n == 1 else x_sb
                for t in range(TT):
                    dve.tensor_scalar(h_tok[:, t, :], src[:, t, :], rstd[:, t:t + 1], None, ALU.mult)\
                       .then_inc(htok_done.sem, 1)

            def norm_gain_lo(l, n):
                dst_hi, dst_lo = (hm_hi, hm_lo) if n == 1 else (act_hi, act_lo)
                for b in range(4):
                    key = ("norm", n, b)
                    dve.wait_ge(*norm_hi.at(l, 4 * n + b + 1))
                    for kk in range(2):
                        k = 2 * b + kk
                        c = PC_NORM[n] + k
                        ins = dve.scalar_tensor_tensor(dst_lo[:, k, :], bank(key)[:, kk * SEQ:(kk + 1) * SEQ],
                                                       par[:, c:c + 1], dst_hi[:, k, :].bitcast(F32),
                                                       ALU.mult, ALU.subtract)
                    ins.then_inc(free(key), 1)

            def rope(l, key, src, n_heads, t, dst, copies):
                shape = [P, n_heads, HD]
                src = src.rearrange("p (h d) -> p h d", d=HD)
                a0 = tmp[:, 0, 0:n_heads * HD].rearrange("p (h d) -> p h d", d=HD)
                a1 = tmp[:, 1, 0:n_heads * HD].rearrange("p (h d) -> p h d", d=HD)
                hf = HD // 2
                half_shape = [P, n_heads, hf]
                steps.mark(dve.tensor_tensor(a0, src, cos2[:, t:t + 1, :].to_broadcast(shape), ALU.mult))
                steps.mark(dve.tensor_tensor(a1[:, :, 0:hf], src[:, :, hf:HD],
                                             sin2[:, t:t + 1, 0:hf].to_broadcast(half_shape), ALU.mult))
                steps.mark(dve.tensor_tensor(a1[:, :, hf:HD], src[:, :, 0:hf],
                                             sin2[:, t:t + 1, hf:HD].to_broadcast(half_shape), ALU.mult))
                steps.settle()
                if copies == 1:
                    dve.tensor_tensor(dst.rearrange("p (h d) -> p h d", d=HD), a0, a1, ALU.add)\
                       .then_inc(roped.sem, 1)
                    return
                dst = dst.rearrange("p (h c d) -> p h c d", c=copies, d=HD)
                steps.mark(dve.tensor_tensor(dst[:, :, 0, :], a0, a1, ALU.add))
                dve.tensor_tensor(dst[:, :, 1, :], a0, a1, ALU.add).then_inc(roped.sem, 1)

            def softplus_dt(l, u):
                n = TT * SSD_HEADS
                key = (u, 0)
                shape = [P, TT, SSD_HEADS]
                row = [sp[:, i, :] for i in range(6)]
                bias = par[:, PC_DTB:PC_DTB + SSD_HEADS].unsqueeze(1).to_broadcast(shape)
                dve.tensor_tensor(row[2].rearrange("p (t h) -> p t h", t=TT),
                                  bank(key)[:, 0:n].rearrange("p (t h) -> p t h", t=TT), bias, ALU.add)\
                   .then_inc(free(key), 1)
                dve.wait_ge(*is_read(l, key))
                dve.scalar_tensor_tensor(row[0], row[2], -1.0, row[2], ALU.mult, ALU.max)\
                   .then_inc(sp_arg.sem, 1)
                dve.wait_ge(*sp_arg.at(l, 1))
                steps.link(dve.tensor_scalar(row[2], row[2], 0.0, None, ALU.max))
                dve.wait_ge(*sp_exp.at(l, 1))
                steps.link(dve.tensor_scalar(row[3], row[1], 2.0, None, ALU.add))
                steps.link(dve.reciprocal(row[4], row[3]))
                steps.link(dve.tensor_tensor(row[3], row[1], row[4], ALU.mult))
                steps.link(dve.tensor_tensor(row[4], row[3], row[3], ALU.mult))
                steps.link(dve.tensor_scalar(row[5], row[4], 1.0 / 17.0, None, ALU.mult))
                for c in (15.0, 13.0, 11.0, 9.0, 7.0, 5.0, 3.0):
                    steps.link(dve.scalar_tensor_tensor(row[5], row[5], 1.0 / c, row[4], ALU.add, ALU.mult))
                steps.link(dve.scalar_tensor_tensor(row[5], row[5], 1.0, row[3], ALU.add, ALU.mult))
                dt_row = dt_sb[:].rearrange("p t h -> p (t h)")
                steps.link(dve.scalar_tensor_tensor(dt_row, row[5], 2.0, row[2], ALU.mult, ALU.add))
                dve.tensor_tensor(a_dt[:], dt_sb[:], par[:, PC_NEGA:PC_DSKIP].unsqueeze(1).to_broadcast(shape),
                                  ALU.mult).then_inc(adt_ready.sem, 1)

            def conv(l, u, j):
                key = (u, 0)
                y, x = two(tmp[:, 0, :]), two(bank(key))
                for tap in (3, 2, 1, 0):
                    s = 3 - tap
                    for m in range(2):
                        wc = PC_CONVW + 12 * tap + 2 * j + m
                        wcol, bcol = half[:, wc:wc + 1], half[:, PC_CONVB + 2 * j + m:PC_CONVB + 2 * j + m + 1]
                        if tap == 3:
                            ins = dve.tensor_scalar(y[:, m, :], x[:, m, :], wcol, bcol, ALU.mult, ALU.add)
                        else:
                            ins = dve.scalar_tensor_tensor(y[:, m, s:SEQ], x[:, m, 0:SEQ - s], wcol, y[:, m, s:SEQ],
                                                           ALU.mult, ALU.add)
                        if tap or not m:
                            steps.mark(ins)
                    if tap:
                        steps.settle()
                ins.then_inc(conv_done.sem, 1)
                dve.wait_ge(*conv_tanh.at(l, j + 1))
                steps.settle()
                dve.wait_ge(*conv_done.at(l, j + 1))
                dve.scalar_tensor_tensor(xbcT[:, 2 * j:2 * j + 2, :], two(tmp[:, 1, :]), 1.0, y, ALU.add, ALU.mult)\
                   .then_inc(xbc_ready.sem, 1)

            def evacuate(l, u):
                w, j = UNITS[u], UNITS[u]["index"]
                kind = w["kind"]
                if not w["last"] or kind in ("qkb", "vb", "kx", "qx", "vx", "gate"):
                    return
                dve.wait_ge(*unit_done.at(l, u + 1))
                if kind == "qa":
                    for t in range(TT):
                        key = unit_bank(u, t)
                        rope(l, key, bank(key), HEADS, t, qk_tok[:, t, 0:512], 1)
                        dve.tensor_copy(mark_sb[:, 0:1], bank(key)[:, 0:1]).then_inc(free(key), 1)
                        steps.settle()
                        dve.wait_ge(*is_read(l, key))
                        dve.wait_ge(*roped.at(l, t + 1))
                elif kind == "kva":
                    src = bank((u, 0))
                    for t in range(TT):
                        steps.mark(dve.tensor_copy(v_a[:, t, :], src[:, t * SEQ + P:(t + 1) * SEQ]))
                        rope(l, (u, 0), src[:, t * SEQ:t * SEQ + P], SWA_KV, t, qk_tok[:, t, 512:768], 2)
                        steps.settle()
                        dve.wait_ge(*roped.at(l, 3 + t))
                    dve.tensor_copy(mark_sb[:, 0:1], src[:, 0:1]).then_inc(free((u, 0)), 1)
                elif kind == "dt":
                    softplus_dt(l, u)
                elif kind == "xbc":
                    conv(l, u, j)
                    dve.tensor_copy(mark_sb[:, 0:1], bank((u, 0))[:, 0:1]).then_inc(free((u, 0)), 1)
                elif kind == "z":
                    for t in range(TT):
                        key = unit_bank(u, t)
                        dve.wait_ge(*z_tanh.at(l, 2 * j + t + 1))
                        dve.scalar_tensor_tensor(z_sb[:, t, 512 * j:512 * j + 512], tmp[:, t, :], 1.0, bank(key),
                                                 ALU.add, ALU.mult).then_inc(free(key), 1)
                elif kind in ("branch_a", "branch_b", "branch_c"):
                    for i, key in enumerate(unit_banks(u, w)):
                        c = w["col"] // P + 2 * i
                        g, mg = g_sb[:, c:c + 2, :], mg_sb[:, c:c + 2, :]
                        if i == 0:
                            wait_read(dve, l, [(v, 0) for v in range(u - 8, u) if UNITS[v]["kind"] == "gate"])
                        if kind == "branch_a":
                            dve.scalar_tensor_tensor(mg, g, 1.0, two(bank(key)), ALU.add, ALU.mult)\
                               .then_inc(free(key), 1)
                            continue
                        part = two(tmp[:, i, :])
                        dve.scalar_tensor_tensor(part, g, 1.0, two(bank(key)), ALU.add, ALU.mult)\
                           .then_inc(free(key), 1)
                        dve.wait_ge(*is_read(l, key))
                        steps.settle()
                        ins = dve.tensor_tensor(mg, mg, part, ALU.add)
                        if kind == "branch_b":
                            steps.mark(ins)
                        else:
                            ins.then_inc(mg_ready.sem, 1)
                            dve.wait_ge(*mg_ready.at(l, j + 1))
                elif kind in ("mix", "co", "down"):
                    if kind == "down":
                        j = j % 2
                    for t in range(TT):
                        key = unit_bank(u, t)
                        xs = x_sb[:, t, 512 * j:512 * j + 512]
                        dve.tensor_tensor(xs, xs, bank(key), ALU.add).then_inc(free(key), 1)
                    if j == 1:
                        for t in range(TT):
                            dve.wait_ge(*is_read(l, unit_bank(u, t)))
                        dve.memset(mark_sb[:, 0:1], 0.0).then_inc(x_ready.sem, 1)
                        dve.wait_ge(*x_ready.at(l, {"mix": 1, "co": 2, "down": 3}[kind]))
                elif kind == "up":
                    dve.wait_ge(*is_read(l, (u, 0)))
                    steps.mark(dve.tensor_tensor(pT_sb[:, j % 2, :], tmp[:, j % 2, :], tmp[:, j % 2, :], ALU.mult))

            def merged_lo(l, j):
                dve.wait_ge(*mg_hi.at(l, j + 1))
                cs = slice(2 * j, 2 * j + 2)
                dve.scalar_tensor_tensor(act_lo[:, cs, :], mg_sb[:, cs, :], 0.5, act_hi[:, cs, :].bitcast(F32),
                                         ALU.mult, ALU.subtract).then_inc(mg_lo.sem, 1)

            def relu_low(l, j):
                steps.settle()
                dve.wait_ge(*relu_h.at(l, j + 1))
                f, m = (j // 2) % 2, slice(2 * (j % 2), 2 * (j % 2) + 2)
                dve.tensor_tensor(relu_lo[:, f, m, :], two(pT_sb[:, j % 2, :]), relu_hi[:, f, m, :].bitcast(F32),
                                  ALU.subtract).then_inc(relu_l.sem, 1)

            def job_mask(l, n):
                branch, t, j = job_of(n)
                key = ("score", n)
                dve.wait_ge(*is_full(l, key))
                if 2 <= n < 18:
                    dve.wait_ge(*is_full(l, ("probsT", n - 2)))
                elif n >= 18:
                    dve.wait_ge(*values_done.at(l, n - 1))
                if branch == 2:
                    if n == 16:
                        dve.wait_ge(*decay_arg.at(l, 1))
                    for i in range(4):
                        h = 4 * j + i
                        ins = dve.scalar_tensor_tensor(s_sb[:, n % 2, i * P:(i + 1) * P], bank(key)[:, i * P:(i + 1) * P],
                                                       acs[:, t, h:h + 1], mask_ssd[:], ALU.subtract, ALU.min)
                    ins.then_inc(free(key), 1)
                    return
                dve.wait_ge(*masked.at(l, n))
                dve.memset(mark_sb[:, 1 + n:2 + n], 0.0)
                keys = (t + 1) * P
                mask = (mask_swa, mask_moba)[branch][:, 2 * P - keys:2 * P]
                for i in range(2):
                    c = i * 2 * P
                    ins = dve.tensor_tensor_reduce(s_sb[:, n % 2, c:c + keys], bank(key)[:, c:c + keys], mask, 1.0,
                                                   -3.0e38, ALU.add, ALU.max, row_max[:, i:i + 1])
                    if i == 0:
                        steps.mark(ins)
                ins.then_inc(free(key), 1)
                steps.settle()
                dve.wait_ge(*is_read(l, key))
                if branch == 0:
                    c = PC_SINK + head_of(j, 0)
                    steps.link(dve.tensor_tensor(row_max[:], row_max[:], par[:, c:c + 3:2], ALU.max))
                h = HEADS * t + head_of(j, 0)
                dve.tensor_scalar(neg_max[:, branch, h:h + 3:2], row_max[:], -ATT_SCALE, None, ALU.mult)\
                   .then_inc(masked.sem, 1)
                if branch == 0 and j == 3:
                    dve.wait_ge(*masked.at(l, n + 1))
                    dve.scalar_tensor_tensor(sink_e[:], par[:, PC_SINK:PC_ALL], ATT_SCALE,
                                             neg_max[:, 0, HEADS * t:HEADS * (t + 1)], ALU.mult, ALU.add)\
                       .then_inc(sink_arg.sem, 1)

            def job_weigh(l, n):
                if not 16 <= n < NJOBS:
                    return
                _, c, q = job_of(n)
                if n == 16:
                    dve.wait_ge(*is_read(l, ("cb",)))
                dve.wait_ge(*exp_done.at(l, n + 1))
                i = SSD_GROUPS * c + q // 2
                s = s_sb[:, n % 2, :].rearrange("p (h k) -> p h k", k=P)
                dve.tensor_tensor(s, s, cbT[:, i:i + 1, :].to_broadcast([P, 4, P]), ALU.mult).then_inc(weighed.sem, 1)

            def close(l, i):
                job, branch, t, g = CLOSINGS[i]
                dve.wait_ge(*values_done.at(l, job + 1))
                if i:
                    dve.wait_ge(*is_full(l, ("closeT", i - 1)))
                y3 = y_tok[:].rearrange("p (h d) -> p h d", d=HD)
                if branch < 2:
                    key = ("values", job - 3)
                    src = bank(key).rearrange("p (h d) -> p h d", d=HD)
                    d = den[:, branch, HEADS * t:HEADS * (t + 1)]
                    if branch == 0:
                        dve.wait_ge(*sink_exp.at(l, t + 1))
                        steps.link(dve.tensor_tensor(d, d, sink_e[:], ALU.add))
                    steps.link(dve.reciprocal(rden[:], d))
                    dve.tensor_tensor(y3, src, wide(rden[:], HD), ALU.mult).then_inc(free(key), 1)
                    return
                key = ("values", job - 1)
                dve.tensor_tensor(y_tok[:], bank(key), xd_sb[:, g, t, :], ALU.add).then_inc(free(key), 1)
                dve.wait_ge(*is_read(l, key))
                if t == 1:
                    key = ("yoff", g)
                    dve.wait_ge(*is_full(l, key))
                    dve.tensor_tensor(tmp[:, 1, :].rearrange("p (h d) -> p h d", d=HD),
                                      bank(key).rearrange("p (h d) -> p h d", d=HD),
                                      wide(decay[:, 1, 8 * g:8 * g + 8], HD), ALU.mult).then_inc(free(key), 1)
                    dve.wait_ge(*is_read(l, key))
                    steps.link(dve.tensor_tensor(y_tok[:], y_tok[:], tmp[:, 1, :], ALU.add))
                dve.scalar_tensor_tensor(y_tok[:], y_tok[:], 0.5, z_sb[:, t, 512 * g:512 * (g + 1)],
                                         ALU.mult, ALU.mult).then_inc(ssd_y.sem, 1)

            def close_lo_part(l, i):
                _, branch, t, g = CLOSINGS[i]
                key = ("closeT", i)
                dve.wait_ge(*close_hi.at(l, i + 1))
                ts = slice(t * P, (t + 1) * P)
                if branch < 2:
                    d_hi, d_lo = ((ya_hi, ya_lo), (yb_hi, yb_lo))[branch]
                    dve.tensor_tensor(d_lo[:, :, ts], bank(key).rearrange("p (k n) -> p k n", n=P),
                                      d_hi[:, :, ts].bitcast(F32), ALU.subtract).then_inc(free(key), 1)
                    return
                for k in range(4):
                    c = PC_SSDN + 4 * g + k
                    ins = dve.scalar_tensor_tensor(yc_lo[:, 4 * g + k, ts], bank(key)[:, k * P:(k + 1) * P],
                                                   par[:, c:c + 1], yc_hi[:, 4 * g + k, ts].bitcast(F32),
                                                   ALU.mult, ALU.subtract)
                ins.then_inc(free(key), 1)

            def sums_of_adt(l):
                key = ("acs",)
                n = SSD_HEADS
                dve.wait_ge(*is_full(l, key))
                steps.link(dve.tensor_copy(acs[:].rearrange("p t h -> p (t h)"), bank(key)[:, 0:2 * n]))
                dve.tensor_tensor(decay[:, 0, :], bank(key)[:, 2 * n:3 * n], acs[:, 0, :], ALU.subtract)\
                   .then_inc(free(key), 1)
                dve.tensor_copy(decay[:, 1, :], acs[:, 1, :]).then_inc(decay_arg.sem, 1)

            def xs_tokens(l, g):
                if g == 0:
                    dve.wait_ge(*values_done.at(l, 8))
                for t in range(TT):
                    dve.wait_ge(*is_full(l, ("xs", g, t)))
                for t in range(TT):
                    key = ("xs", g, t)
                    src = bank(key).rearrange("p (h d) -> p h d", d=HD)
                    hs = slice(8 * g, 8 * g + 8)
                    steps.mark(dve.tensor_tensor(xdt[:, t, 512 * g:512 * (g + 1)].rearrange("p (h d) -> p h d", d=HD),
                                                 src, wide(dt_sb[:, t, hs], HD), ALU.mult))
                    dve.tensor_tensor(xd_sb[:, g, t, :].rearrange("p (h d) -> p h d", d=HD), src,
                                      wide(par[:, PC_DSKIP + 8 * g:PC_DSKIP + 8 * g + 8], HD), ALU.mult)\
                       .then_inc(free(key), 1)

            with dve.Fori(0, DEPTH) as l:
                steps.enter(l)
                steps.mark(dve.tensor_copy(par[:], cols[:, l, :]))
                dve.tensor_scalar(half[:], cols[:, l, 0:PC_ROWS], 0.5, None, ALU.mult).then_inc(par_ready.sem, 1)
                steps.settle()
                dve.wait_ge(*par_ready.at(l, 1))
                norm_scale(l, 0)
                lo(l, 0)
                norm_gain_lo(l, 0)
                lo(l, 1)
                lo(l, 2)
                for u, w in enumerate(UNITS):
                    n, h = u - JOB_SLOT0, u - CROSS_SLOT0
                    if 0 <= n < NJOBS:
                        job_mask(l, n)
                    job_weigh(l, n - 1)
                    if u == ACS_SLOT:
                        sums_of_adt(l)
                    if u in (XS_SLOT, XS_SLOT + 1):
                        xs_tokens(l, u - XS_SLOT)
                    if u == XS_SLOT + 1:
                        dve.wait_ge(*decay_exp.at(l, 1))
                        steps.settle()
                        dve.tensor_tensor(xdec[:].rearrange("p (h d) -> p h d", d=HD),
                                          xdt[:, 0, :].rearrange("p (h d) -> p h d", d=HD),
                                          wide(decay[:, 0, :], HD), ALU.mult).then_inc(xdec_ready.sem, 1)
                    for i in range(8):
                        if u == CLOSE_SLOT[i] + 1:
                            close_lo_part(l, i)
                    for i in range(8):
                        if u == CLOSE_SLOT[i]:
                            close(l, i)
                    if 0 <= h < X_HEADS:
                        if h:
                            dve.wait_ge(*is_read(l, ("xscore", h - 1)))
                        dve.wait_ge(*is_full(l, ("xscore", h)))
                        steps.link(dve.tensor_reduce(xmax[:], two(bank(("xscore", h))), AX.X, ALU.max))
                        dve.tensor_scalar(xmax[:], xmax[:], -X_SCALE, None, ALU.mult).then_inc(xmax_ready.sem, 1)
                    evacuate(l, u)
                    if w["kind"] == "branch_c":
                        merged_lo(l, w["index"])
                    if u + RING < NU:
                        lo(l, u + RING)
                    if w["kind"] == "up":
                        relu_low(l, w["index"])
                    if 0 <= h < X_HEADS:
                        dve.wait_ge(*is_read(l, ("xscore", h)))
                        steps.link(dve.reciprocal(row_max[:], xden[:]))
                        for t in range(TT):
                            s = s_sb[:, h % 2, t * SEQ:(t + 1) * SEQ]
                            ins = dve.tensor_scalar(s, s, row_max[:, t:t + 1], None, ALU.mult)
                            if t == 0:
                                steps.mark(ins)
                        ins.then_inc(xprobs.sem, 1)
                    for hh in {U_VX + 2: (0, 1), U_VX + 3: (2, 3)}.get(u, ()):
                        dve.wait_ge(*xo_hi.at(l, hh + 1))
                        cs = slice(2 * hh, 2 * hh + 2)
                        dve.tensor_tensor(o_lo[:, cs, :], two(bank(("xvalues", hh))), o_hi[:, cs, :].bitcast(F32),
                                          ALU.subtract).then_inc(free(("xvalues", hh)), 1)
                    for n in (1, 2, 3):
                        if u == NORM_SCALE_SLOT[n]:
                            norm_scale(l, n)
                        if u == NORM_TURN_SLOT[n]:
                            norm_gain_lo(l, n)
                steps.leave(DEPTH)
            dve.wait_ge(rstd_fin, 1)
            dve.wait_ge(gain_loaded, 16)
            for t in range(TT):
                dve.scalar_tensor_tensor(h_tok[:, t, :], x_sb[:, t, :], rstd[:, t:t + 1], gain[:], ALU.mult,
                                         ALU.mult).then_inc(fin_ready, 1)


_INS = ["x", "mem", "positions", "norm_mix", "w_in", "w_gate", "b_gate", "swa_sinks", "conv_w", "conv_b", "dt_bias",
        "a_log", "d_skip", "ssd_norm", "w_br_swa", "w_br_moba", "w_br_ssd", "w_mix_out", "norm_cross", "norm_mem",
        "w_cq", "w_ckv", "w_co", "norm_mlp", "w_up", "w_down", "final_norm"]


def kernel(**inputs):
    import concourse.bacc as bacc
    from concourse.bass_utils import run_bass_kernel_spmd

    nc = bacc.Bacc("TRN2", target_bir_lowering=False, num_devices=1)
    arrays, args = {}, {}
    for name in _INS:
        arr = np.ascontiguousarray(inputs[name])
        arrays[f"in_{name}_dram"] = arr
        args[name] = nc.dram_tensor(f"in_{name}_dram", arr.shape, mybir.dt.from_np(arr.dtype),
                                    kind="ExternalInput").ap()
    out = nc.dram_tensor("out_0_dram", (1, SEQ, D), F32, kind="ExternalOutput").ap()
    trunk(nc, args, out)
    r = run_bass_kernel_spmd(nc, [arrays], core_ids=[0])
    return r.results[0]["out_0_dram"]
```

```python
import math
from contextlib import ExitStack

import numpy as np
import concourse.bass as bass
from concourse import mybir

F32 = mybir.dt.float32
F32R = mybir.dt.float32r
I32 = mybir.dt.int32
ALU = mybir.AluOpType
ACT = mybir.ActivationFunctionType
AX = mybir.AxisListType

P = 128
D = 1024
SEQ = 256
DEPTH = 2
KT = D // P
TT = SEQ // P
EPS = 1e-6
HD = 64
HEADS = 8
SWA_KV = 2
SSD_HEADS = 16
SSD_GROUPS = 2
ROPE_THETA = 150000.0
X_HEADS = 4
D_FF = 4 * D
FF_BLOCKS = D_FF // 512
NEG = -1.0e30
ATT_SCALE = HD ** -0.5
X_SCALE = (D // X_HEADS) ** -0.5

C_QA, C_KVA, C_QB, C_KB, C_VB, C_Z, C_XBC, C_DT = 0, 512, 768, 1280, 1792, 2304, 3328, 4864

PC_NORM = [0, 16, 8, 24]
PC_SSDN, PC_CONVW, PC_CONVB, PC_BGATE, PC_ROWS = 32, 40, 88, 100, 124
PC_DTB, PC_EXPA, PC_DSKIP, PC_SINK, PC_ALL = 124, 140, 156, 172, 180

CUT = 1536
RING = 3


def make_units():
    units = []

    def unit(kind, orient, weight, row, k_tiles, col, cols, act, index, part=0, first=True, last=True):
        units.append(dict(kind=kind, orient=orient, weight=weight, row=row, kt=k_tiles, col=col, cols=cols,
                          act=act, index=index, first=first, last=last, opens=len(units) - part))

    def stripe_b(kind, weight, col, cols, act, j, k_tiles=(4, 4)):
        for part, kt in enumerate(k_tiles):
            unit(kind, "B", weight, P * sum(k_tiles[:part]), kt, col, cols, act, j, part, part == 0,
                 part == len(k_tiles) - 1)

    def stripes_b(kind, weight, col, act, n):
        for j in range(n):
            stripe_b(kind, weight, col + 512 * j, 512, act, j)

    def stripes_a(kind, weight, col, act, n):
        for j in range(n):
            unit(kind, "A", weight, 0, 8, col + 256 * j, 256, act, j)

    def xbc(j):
        unit("xbc", "A", "w_in", 0, 8, C_XBC + 256 * j, 256, "h", j)

    stripes_b("qa", "w_in", C_QA, "h", 1)
    for j in range(4):
        unit("qkb", "A", "w_in", 0, 8, C_QB + 256 * j, 256, "h", j)
        if j == 0:
            stripe_b("kva", "w_in", C_KVA, 256 + SSD_HEADS, "h", 0, (2, 3, 3))
        if j < 3:
            xbc(j)
    stripes_b("vb", "w_in", C_VB, "h", 1)
    for j in range(2):
        xbc(3 + j)
        stripe_b("z", "w_in", C_Z + 512 * j, 512, "h", j)
    xbc(5)
    stripes_a("gate", "w_gate", 0, "h", 4)
    for j in range(2):
        unit("branch_a", "A", "w_br_swa", 0, 4, 512 * j, 512, "y_swa", j)
    stripes_a("gate", "w_gate", D, "h", 4)
    for j in range(2):
        unit("branch_b", "A", "w_br_moba", 0, 4, 512 * j, 512, "y_moba", j)
    stripes_a("gate", "w_gate", 2 * D, "h", 4)
    stripes_a("branch_c", "w_br_ssd", 0, "y_ssd", 4)
    stripes_b("mix", "w_mix_out", 0, "merged", 2)
    stripes_a("kx", "w_ckv", 0, "mem", 4)
    stripes_a("qx", "w_cq", 0, "hq", 4)
    stripes_b("vx", "w_ckv", D, "mem", 2)
    stripes_b("co", "w_co", 0, "o", 2)

    def up(f):
        for j in range(2):
            unit("up", "A", "w_up", 0, 8, 512 * f + 256 * j, 256, "hf", 2 * f + j)

    def down(f):
        for j in range(2):
            unit("down", "B", "w_down", 512 * f, 4, 512 * j, 512, "relu", 2 * f + j, 0,
                 f == 0, f == FF_BLOCKS - 1)

    up(0)
    for f in range(FF_BLOCKS - 1):
        up(f + 1)
        down(f)
    down(FF_BLOCKS - 1)
    return units


UNITS = make_units()
NU = len(UNITS)
assert NU % RING == 0


def first_of(kind, index=0):
    return next(u for u, w in enumerate(UNITS) if w["kind"] == kind and w["index"] == index)


U_QA, U_KVA, U_VB = (first_of(k) for k in ("qa", "kva", "vb"))
U_XBC = [first_of("xbc", j) for j in range(6)]
U_Z = [first_of("z", j) for j in range(2)]
U_SWA = U_KVA + 2
U_GATE, U_BRA, U_BRB, U_BRC, U_MIX = (first_of(k) for k in ("gate", "branch_a", "branch_b", "branch_c", "mix"))
U_KX, U_QX, U_VX, U_CO, U_UP = (first_of(k) for k in ("kx", "qx", "vx", "co", "up"))

JOB_SLOT0 = U_SWA + 2
NJOBS = 24
SSD_JOB0, SSD_PAUSE = 16, 2


def job_slot(n):
    return JOB_SLOT0 + n + (SSD_PAUSE if n >= SSD_JOB0 else 0)


def job_at(s):
    return next((n for n in range(NJOBS) if job_slot(n) == s), -1)


SWA_T_SLOT = U_SWA + 1
DT_SLOT = U_VB + 1
ACS_SLOT, BTOK_SLOT, CB_SLOT, STATES_SLOT = U_XBC[3], U_XBC[4] + 2, U_XBC[5] + 3, U_XBC[5] + 6
XS_SLOTS = (U_Z[0] + 1, U_XBC[5] + 2)
MEM_SQUARE_SLOT, MEM_SCALE_SLOT = U_BRC + 1, U_BRC + 2
NORM_TURN_SLOT = {1: U_MIX, 2: U_QX - 2}
PAIRS = (U_QA, U_CO + 2, NU - 2)
CROSS_SLOT0 = U_QX + 1


def job_of(n):
    return n // 8, (n % 8) // 4, n % 4


def head_of(j, i):
    return 4 * (j // 2) + j % 2 + 2 * i


CLOSINGS = [(3, 0, 0, 0), (7, 0, 1, 0), (11, 1, 0, 0), (15, 1, 1, 0),
            (17, 2, 0, 0), (19, 2, 0, 1), (21, 2, 1, 0), (23, 2, 1, 1)]
CLOSE_SLOT = [job_slot(c[0]) + 2 for c in CLOSINGS]

SB_, TB_, OB_, YB_ = 4, 5, 6, 7


def unit_banks(u, w):
    if w["kind"] == "down":
        return [("down", 2 * (w["index"] % 2) + t) for t in range(TT)]
    if w["orient"] == "B":
        return [(w["opens"], t) for t in range(TT)]
    return [(u, i) for i in range(w["cols"] // 256)]


def slot_banks(s):
    out = []
    if s == SWA_T_SLOT:
        out += [(b, ("qkT", i)) for i, b in enumerate((SB_, TB_, OB_))]
    if 0 <= job_at(s) < SSD_JOB0:
        out.append((SB_, ("score", job_at(s))))
    if 0 <= job_at(s - 1) < SSD_JOB0:
        out.append((TB_, ("probsT", job_at(s - 1))))
    if job_at(s - 2) in [0, 4, 8, 12, 16, 18, 20, 22]:
        out.append((OB_, ("values", job_at(s - 2))))
    if s == ACS_SLOT:
        out.append((YB_, ("acs",)))
    if s == CB_SLOT:
        out.append((YB_, ("cb",)))
    if s == BTOK_SLOT:
        out.append((YB_, ("btok",)))
    if s in XS_SLOTS:
        out += [(YB_, ("xs", XS_SLOTS.index(s), 0)), (SB_, ("xs", XS_SLOTS.index(s), 1))]
    if s == STATES_SLOT:
        out += [(YB_, ("states", 0)), (SB_, ("states", 1))]
    for i, (_, branch, tile, group) in enumerate(CLOSINGS):
        if branch == 2 and tile == 1 and s == CLOSE_SLOT[i]:
            out.append((YB_, ("yoff", group)))
    for i in range(8):
        if s == CLOSE_SLOT[i] + 1:
            out.append((YB_, ("closeT", i)))
    for n in (1, 2):
        if s == NORM_TURN_SLOT[n]:
            out += [(SB_ + b, ("norm", n, b)) for b in range(4)]
    if s in (U_CO + 2, U_CO + 3):
        out += [(SB_ + b, ("norm", 3, b)) for b in ((0, 1), (2, 3))[s - U_CO - 2]]
    h = s - CROSS_SLOT0
    if 0 <= h < X_HEADS:
        out.append((SB_, ("xscore", h)))
    if 0 <= h - 1 < X_HEADS:
        out.append((TB_, ("xprobsT", h - 1)))
    if s == U_VX + 2:
        out += [(OB_, ("xvalues", 0)), (YB_, ("xvalues", 1))]
    if s == U_VX + 3:
        out += [(OB_, ("xvalues", 2)), (YB_, ("xvalues", 3))]
    return out


def make_banks():
    where, uses, turn = {}, [0] * 8, 0

    def use(bank, key):
        where[key] = (bank, uses[bank])
        uses[bank] += 1

    for b in range(4):
        use(SB_ + 2 * (b % 2) + b // 2, ("norm", 0, b))
    for u, w in enumerate(UNITS):
        for key in unit_banks(u, w):
            if key in where:
                continue
            if w["kind"] == "down":
                use(SB_ + key[1], key)
            else:
                use(turn % 4, key)
                turn += 1
        for bank, key in slot_banks(u):
            use(bank, key)
    return where, uses


BANK_OF, BANK_USES = make_banks()
DVE_STEPS = 142


class Signal:

    def __init__(self, sem, per_layer, credit=0):
        self.sem, self.per_layer, self.credit = sem, per_layer, credit

    def at(self, l, n):
        assert n + self.credit > 0
        return self.sem, l * self.per_layer + (n + self.credit)


class Steps:

    def __init__(self, eng, sem, per_layer):
        self.eng, self.sem, self.per_layer = eng, sem, per_layer
        self.before, self.n, self.l = 0, 0, 0

    def enter(self, l):
        self.before, self.n, self.l = self.before + self.n, 0, l

    def leave(self, layers):
        assert self.n == self.per_layer, f"{self.sem}: {self.n} steps a layer"
        self.before, self.n, self.l = self.before + layers * self.n, 0, 0

    def mark(self, ins):
        ins.then_inc(self.sem, 1)
        self.n += 1

    def settle(self):
        self.eng.wait_ge(self.sem, self.l * self.per_layer + (self.before + self.n))

    def link(self, ins):
        self.mark(ins)
        self.settle()


def trunk(nc, a, out):
    ctx = ExitStack()
    with ctx:
        top = [-(-nc.sbuf_base // 64) * 64]

        def at(name, shape, dtype, offset):
            return nc.alloc_sbuf_tensor_at(name, shape, dtype, offset=offset)

        def region(n_bytes):
            offset = top[0]
            top[0] += n_bytes
            assert top[0] <= nc.sbuf_usable_end, top[0]
            return offset

        def keep(name, shape, dtype=F32):
            size = int(np.prod(shape[1:])) * 4
            return at(name, shape, dtype, region(-(-size // 32) * 32))

        raw = keep("raw", [P, RING, 2048])
        w_hi = keep("w_hi", [P, RING, 2048], F32R)
        w_lo = keep("w_lo", [P, RING, 2048], F32R)
        x_sb = keep("x_sb", [P, TT, D])
        act_hi = keep("act_hi", [P, KT, SEQ], F32R)
        act_lo = keep("act_lo", [P, KT, SEQ], F32R)

        r_a = region(8192)
        qk_tok = at("qk_tok", [P, TT, 768], F32, r_a)
        z_sb = at("z_sb", [P, TT, D], F32, r_a)
        mem_sb = at("mem_sb", [P, TT, D], F32, r_a)
        rows = at("rows", [P, DEPTH, P], F32, r_a)
        r_b = region(8192)
        qkT_a = at("qkT_a", [P, 6, SEQ], F32, r_b)
        v_a = at("v_a", [P, TT, P], F32, r_b + 6144)
        xdt = at("xdt", [P, TT, D], F32, r_b)
        v_x = at("v_x", [P, TT, D], F32, r_b)
        r_c = region(16384)
        qkT_b = at("qkT_b", [P, 8, SEQ], F32, r_c)
        v_b = at("v_b", [P, TT, 512], F32, r_c + 8192)
        h_tok = at("h_tok", [P, TT, D], F32, r_c)
        gain = at("gain", [P, D], F32, r_c + 8192)
        yc_hi = at("yc_hi", [P, KT, SEQ], F32R, r_c)
        yc_lo = at("yc_lo", [P, KT, SEQ], F32R, r_c + 8192)
        hm_hi = at("hm_hi", [P, KT, SEQ], F32R, r_c)
        hm_lo = at("hm_lo", [P, KT, SEQ], F32R, r_c + 8192)
        r_d = region(8192)
        ya_hi = at("ya_hi", [P, 4, SEQ], F32R, r_d)
        ya_lo = at("ya_lo", [P, 4, SEQ], F32R, r_d + 4096)
        q_xT = at("q_xT", [P, KT, SEQ], F32, r_d)
        r_e = region(8192)
        yb_hi = at("yb_hi", [P, 4, SEQ], F32R, r_e)
        yb_lo = at("yb_lo", [P, 4, SEQ], F32R, r_e + 4096)
        pT_x = at("pT_x", [P, X_HEADS, TT, SEQ], F32, r_e)
        r_f = region(12288)
        xbcT = at("xbcT", [P, 12, SEQ], F32, r_f)
        xd_sb = at("xd_sb", [P, SSD_GROUPS, TT, 512], F32, r_f)
        k_xT = at("k_xT", [P, KT, SEQ], F32, r_f)
        r_g = region(16384)
        g_sb = at("g_sb", [P, KT, SEQ], F32, r_g)
        mg_sb = at("mg_sb", [P, KT, SEQ], F32, r_g + 8192)
        o_hi = at("o_hi", [P, KT, SEQ], F32R, r_g)
        o_lo = at("o_lo", [P, KT, SEQ], F32R, r_g + 8192)
        relu_hi = at("relu_hi", [P, 2, 4, SEQ], F32R, r_g)
        relu_lo = at("relu_lo", [P, 2, 4, SEQ], F32R, r_g + 8192)
        s_sb = keep("s_sb", [P, 2, 512])
        pT_sb = keep("pT_sb", [P, 2, 512])
        y_tok = keep("y_tok", [P, 512])
        tmp = keep("tmp", [P, 2, 512])
        xdec = keep("xdec", [P, D])
        acsT = at("acsT", [SSD_HEADS, SEQ], F32, top[0] - 4 * D)
        states = keep("states", [P, SSD_GROUPS, 512])
        cbT = keep("cbT", [P, TT * SSD_GROUPS, P])
        b_tok = keep("b_tok", [P, SSD_GROUPS, P])

        ident = keep("ident", [P, P])
        tri = keep("tri", [P, P])
        ones = keep("ones", [P, P])
        mask_swa = keep("mask_swa", [P, 2 * P])
        mask_moba = keep("mask_moba", [P, 2 * P])
        mask_ssd = keep("mask_ssd", [P, P])
        cos2 = keep("cos2", [P, TT, HD])
        sin2 = keep("sin2", [P, TT, HD])
        cols = keep("cols", [P, DEPTH, PC_ALL])
        par = keep("par", [P, PC_ALL])
        half = keep("half", [P, PC_ROWS])
        inv_f = keep("inv_f", [P, HD // 2])
        pos_i = keep("pos_i", [P, TT], I32)
        pos_f = keep("pos_f", [P, TT])
        pool_c = keep("pool_c", [P, 7, 2])
        sq = keep("sq", [P, 5, 2])
        ms = keep("ms", [P, 5, 2])
        rstd = keep("rstd", [P, 5, 2])
        neg_max = keep("neg_max", [P, 2, 2 * HEADS])
        row_max = keep("row_max", [P, 2])
        den = keep("den", [P, 2, 2 * HEADS])
        mark_pool = keep("mark_pool", [P, 16])
        mark_sb = keep("mark_sb", [P, 17])
        rden = keep("rden", [P, HEADS])
        sink_e = keep("sink_e", [P, HEADS])
        sp = keep("sp", [P, 6, TT * SSD_HEADS])
        dt_sb = keep("dt_sb", [P, TT, SSD_HEADS])
        a_dt = keep("a_dt", [P, TT, SSD_HEADS])
        acs = keep("acs", [P, TT, SSD_HEADS])
        decay = keep("decay", [P, 2, SSD_HEADS])
        ssq = keep("ssq", [P, 1])
        sms = keep("sms", [P, 1])
        srstd = keep("srstd", [P, 1])
        xmax = keep("xmax", [P, 2])
        xden = keep("xden", [P, 2])

        psum = ctx.enter_context(nc.psum_tensor("psum", [P, 8, 512], F32))

        def sem(name):
            return ctx.enter_context(nc.semaphore(name))

        loads = [2 if w["kind"] == "kva" else 1 for w in UNITS]
        raw_loaded = [Signal(sem(f"raw_loaded{i}"), 16 * sum(loads[i::RING])) for i in range(RING)]
        mem_loaded = Signal(sem("mem_loaded"), 16)
        hi_ready = Signal(sem("hi_ready"), NU)
        lo_ready = Signal(sem("lo_ready"), NU - 1, RING)
        lo_first = Signal(sem("lo_first"), 2)
        unit_done = Signal(sem("unit_done"), NU, RING)
        bank_full = [sem(f"bank_full{b}") for b in range(8)]
        bank_free = [sem(f"bank_free{b}") for b in range(8)]
        par_ready = Signal(sem("par_ready"), 2)
        tile0_done = Signal(sem("tile0_done"), len(PAIRS))
        mem_scaled = Signal(sem("mem_scaled"), TT)
        sq_done = Signal(sem("sq_done"), 8)
        rstd_done = Signal(sem("rstd_done"), 5)
        htok_done = Signal(sem("htok_done"), TT)
        norm_hi = Signal(sem("norm_hi"), 16)
        roped = Signal(sem("roped"), 4)
        masked = Signal(sem("masked"), 16, 1)
        exp_done = Signal(sem("exp_done"), NJOBS)
        weighed = Signal(sem("weighed"), 8)
        values_done = Signal(sem("values_done"), NJOBS)
        sink_arg = Signal(sem("sink_arg"), 2)
        sink_exp = Signal(sem("sink_exp"), 2)
        conv_done = Signal(sem("conv_done"), 6)
        conv_tanh = Signal(sem("conv_tanh"), 6)
        xbc_ready = Signal(sem("xbc_ready"), 6)
        z_tanh = Signal(sem("z_tanh"), 4)
        sp_arg = Signal(sem("sp_arg"), 1)
        sp_exp = Signal(sem("sp_exp"), 1)
        adt_ready = Signal(sem("adt_ready"), 1)
        acs_turned = Signal(sem("acs_turned"), 1)
        acs_stored = Signal(sem("acs_stored"), 16)
        acs_spread = Signal(sem("acs_spread"), 16 * 8)
        decays_made = Signal(sem("decays_made"), 8)
        decay_arg = Signal(sem("decay_arg"), 1)
        decay_exp = Signal(sem("decay_exp"), 1)
        xdec_ready = Signal(sem("xdec_ready"), 1)
        ssd_y = Signal(sem("ssd_y"), 4)
        ssd_sq = Signal(sem("ssd_sq"), 4)
        ssd_rstd = Signal(sem("ssd_rstd"), 4, 1)
        ssd_yn = Signal(sem("ssd_yn"), 4, 1)
        close_hi = Signal(sem("close_hi"), 8)
        mg_ready = Signal(sem("mg_ready"), 4)
        mg_hi = Signal(sem("mg_hi"), 4)
        mg_lo = Signal(sem("mg_lo"), 4)
        xmax_ready = Signal(sem("xmax_ready"), 4)
        xprobs = Signal(sem("xprobs"), 4, 1)
        xo_hi = Signal(sem("xo_hi"), 4)
        relu_h = Signal(sem("relu_h"), 16)
        relu_l = Signal(sem("relu_l"), 16)
        dve_steps = sem("dve_steps")
        heads_loaded = sem("heads_loaded")
        x_loaded, par_loaded, pos_loaded = sem("x_loaded"), sem("par_loaded"), sem("pos_loaded")
        const_made, rows_turned, cols_ready = sem("const_made"), sem("rows_turned"), sem("cols_ready")
        angle_ready, sines_ready = sem("angle_ready"), sem("sines_ready")
        a_exp = Signal(sem("a_exp"), 1)
        gain_loaded, fin_ready, stored = sem("gain_loaded"), sem("fin_ready"), sem("stored")
        pool_steps = Signal(sem("pool_steps"), 18)
        sq_fin, ms_fin, rstd_fin = sem("sq_fin"), sem("ms_fin"), sem("rstd_fin")

        def bank(key):
            return psum[:, BANK_OF[key][0], :]

        def is_free(l, key):
            b, k = BANK_OF[key]
            return bank_free[b], l * BANK_USES[b] + (k + 1)

        def is_full(l, key):
            b, k = BANK_OF[key]
            return bank_full[b], l * FULLS[b] + (FULL_OF[key] + 1)

        def is_read(l, key):
            b, k = BANK_OF[key]
            return bank_free[b], l * BANK_USES[b] + (k + 2)

        def wait_lo(eng, l, u):
            if u % NU == 0:
                eng.wait_ge(*lo_first.at(l, 2))
            else:
                eng.wait_ge(*lo_ready.at(l, u))

        def x_left(eng, l, t):
            for j in range(2):
                b, k = BANK_OF[("down", 2 * j + t)]
                assert k == BANK_USES[b] - 1
                eng.wait_ge(bank_free[b], l * BANK_USES[b] + 1)

        def wait_read(eng, l, keys):
            last = {}
            for key in keys:
                b, k = BANK_OF[key]
                if b not in last or k > BANK_OF[last[b]][1]:
                    last[b] = key
            for key in last.values():
                eng.wait_ge(*is_read(l, key))

        def free(key):
            return bank_free[BANK_OF[key][0]]

        def full(key):
            return bank_full[BANK_OF[key][0]]

        FULL_OF, FULLS = {}, [0] * 8
        for key, (b, k) in sorted(BANK_OF.items(), key=lambda kv: (kv[1][0], kv[1][1])):
            if isinstance(key[0], int) or key[0] in ("down", "values"):
                continue
            FULL_OF[key] = FULLS[b]
            FULLS[b] += 1

        weights = {n: a[n] for n in ("w_in", "w_gate", "w_br_swa", "w_br_moba", "w_br_ssd", "w_mix_out",
                                     "w_cq", "w_ckv", "w_co", "w_up", "w_down")}
        acs_rows = nc.dram_tensor("acs_rows", (DEPTH, TT, SSD_HEADS * P), F32, kind="Internal").ap()
        inv = nc.inline_tensor(
            (np.float32(ROPE_THETA) ** (-np.arange(HD // 2, dtype=np.float32) / np.float32(HD // 2)))
            .astype(np.float32)[None, :], "rope_inverse_frequencies")
        block = ctx.enter_context(nc.Block())

        def prev_user(u):
            return u - RING

        def unit_bank(u, i):
            return unit_banks(u, UNITS[u])[i]

        def wide(ap, n):
            return ap.unsqueeze(2).to_broadcast([P, ap.shape[1], n])

        @block.sync
        def _(sp):
            sp.dma_start(pos_i[:], a["positions"].rearrange("b (t p) -> p (b t)", p=P),
                         allow_slow_non_contiguous=True).then_inc(pos_loaded, 16)
            sp.dma_start(inv_f[:], inv.ap()[0].partition_broadcast(P)).then_inc(pos_loaded, 16)
            sp.dma_start(x_sb[:], a["x"].rearrange("b (t p) d -> p (b t) d", p=P)).then_inc(x_loaded, 16)
            lay = "l (k p) -> k l p"
            for name, r0, n in (("norm_mix", 0, 8), ("norm_cross", 8, 8), ("norm_mem", 16, 8),
                                ("norm_mlp", 24, 8), ("ssd_norm", PC_SSDN, 8), ("conv_b", PC_CONVB, 12),
                                ("b_gate", PC_BGATE, 24)):
                sp.dma_start(rows[r0:r0 + n, :, :], a[name].rearrange(lay, p=P)).then_inc(par_loaded, 16)
            sp.dma_start(rows[PC_CONVW:PC_CONVB, :, :],
                         a["conv_w"].rearrange("l t (c p) -> (t c) l p", p=P)).then_inc(par_loaded, 16)

            with sp.Fori(0, DEPTH) as l:
                for u, w in enumerate(UNITS):
                    if u == U_BRC + 1:
                        sp.wait_ge(*ssd_y.at(l, 4))
                        sp.dma_start(mem_sb[:], a["mem"].rearrange("b (t p) d -> p (b t) d", p=P))\
                          .then_inc(mem_loaded.sem, 16)
                    if u == ACS_SLOT + RING + 1:
                        sp.wait_ge(*acs_turned.at(l, 1))
                        sp.dma_start(acs_rows[l].rearrange("t (h p) -> h t p", p=P),
                                     acsT[:].rearrange("h (t p) -> h t p", p=P)).then_inc(acs_stored.sem, 16)
                    n = job_at(u - RING + 1)
                    if n >= SSD_JOB0:
                        if n == SSD_JOB0:
                            sp.wait_ge(*acs_stored.at(l, 16))
                        if n < SSD_JOB0 + 2:
                            sp.wait_ge(*values_done.at(l, n - 1))
                        else:
                            sp.wait_ge(*decays_made.at(l, n - 1 - SSD_JOB0))
                        _, t, j = job_of(n)
                        sp.dma_start(pT_sb[:, n % 2, :], acs_rows[l, t, 4 * j * P:4 * (j + 1) * P]
                                     .partition_broadcast(P)).then_inc(acs_spread.sem, 16)
                    n = w["kt"] * w["cols"]
                    if u >= RING:
                        wait_lo(sp, l, prev_user(u))
                    else:
                        sp.wait_ge(*lo_ready.at(l, prev_user(u) + 1))
                    dst = raw[:, u % RING, 0:n].rearrange("p (k n) -> p k n", n=w["cols"])
                    src = weights[w["weight"]][l, w["row"]:w["row"] + w["kt"] * P, :]
                    src = src.rearrange("(k p) n -> p k n", p=P)
                    n = w["cols"]
                    if w["kind"] == "kva":
                        n -= SSD_HEADS
                        sp.dma_start(dst[:, :, n:n + SSD_HEADS], src[:, :, C_DT:C_DT + SSD_HEADS])\
                          .then_inc(raw_loaded[u % RING].sem, 16)
                    sp.dma_start(dst[:, :, 0:n], src[:, :, w["col"]:w["col"] + n])\
                      .then_inc(raw_loaded[u % RING].sem, 16)

            sp.wait_ge(*unit_done.at(DEPTH - 1, U_CO))
            sp.dma_start(gain[:], a["final_norm"].partition_broadcast(P)).then_inc(gain_loaded, 16)
            for i in range(2 * TT):
                t, cs = i // 2, slice(512 * (i % 2), 512 * (i % 2) + 512)
                sp.wait_ge(fin_ready, i + 1)
                sp.dma_start(out[0, t * P:(t + 1) * P, cs], h_tok[:, t, cs]).then_inc(stored, 16)
            sp.wait_ge(stored, 16 * 2 * TT)

        @block.gpsimd
        def _(pool):
            POOL_CONSTANTS = (1.0 / D, SSD_GROUPS / D, EPS, -0.5, X_SCALE ** -2 / D, X_SCALE ** -2 * EPS, -1.0)
            NORM_CONSTANTS = ((0, 2, 3), (0, 2, 3), (4, 5, 3), (0, 2, 6), (0, 2, 3))
            pool.memset(pool_c[:, 0, :], POOL_CONSTANTS[0]).then_inc(lo_ready.sem, RING)
            pool.memset(ident[:], 0.0).then_inc(unit_done.sem, RING)
            for name, c0, n in (("dt_bias", PC_DTB, SSD_HEADS), ("a_log", PC_EXPA, SSD_HEADS),
                                ("d_skip", PC_DSKIP, SSD_HEADS), ("swa_sinks", PC_SINK, HEADS)):
                pool.dma_start(cols[:, :, c0:c0 + n], a[name].partition_broadcast(P)).then_inc(heads_loaded, 16)
            credited = [sig.sem for sig in (ssd_rstd, ssd_yn, xprobs, masked)]
            for i, s in enumerate(credited + bank_free):
                pool.memset(mark_pool[:, i:i + 1], 0.0).then_inc(s, 1)
            for i in range(1, 7):
                pool.memset(pool_c[:, i, :], POOL_CONSTANTS[i]).then_inc(const_made, 1)
            for i, (tile, value) in enumerate(((tri, 1.0), (ones, 1.0), (mask_swa, 0.0), (mask_moba, 0.0),
                                               (mask_ssd, 0.0))):
                pool.memset(tile[:], value).then_inc(const_made, 1)
            pool.wait_ge(const_made, 11)
            pool.wait_ge(lo_ready.sem, RING)
            pool.wait_ge(unit_done.sem, RING)

            def select(ap, step, base, channel, op, fill):
                pool.affine_select(out=ap, in_=ap, pattern=[[step, P]], compare_op=op, fill=fill, base=base,
                                   channel_multiplier=channel).then_inc(const_made, 1)

            select(ident[:], 1, 0, -1, ALU.not_equal, 1.0)
            select(tri[:], 1, 0, -1, ALU.is_ge, 0.0)
            select(mask_ssd[:], 1, 0, -1, ALU.is_ge, NEG)
            select(mask_swa[:, 0:P], 1, 0, -1, ALU.is_gt, NEG)
            select(mask_swa[:, P:2 * P], -1, 0, 1, ALU.is_ge, NEG)
            select(mask_moba[:, P:2 * P], -1, 0, 1, ALU.is_ge, NEG)

            def step(sem, value, ins):
                ins.then_inc(sem, 1)
                pool.wait_ge(sem, value)

            def norm(n, t0, t1, first, second, made):
                mean, eps, power = NORM_CONSTANTS[n]
                ts = slice(t0, t1)
                step(*first, pool.tensor_tensor(ms[:, n, ts], sq[:, n, ts], pool_c[:, mean, ts], ALU.mult))
                step(*second, pool.tensor_tensor(ms[:, n, ts], ms[:, n, ts], pool_c[:, eps, ts], ALU.add))
                pool.tensor_tensor(rstd[:, n, ts], ms[:, n, ts], pool_c[:, power, ts], ALU.pow).then_inc(made, 1)

            def weigh(l, n):
                _, c, q = job_of(n)
                if n == SSD_JOB0:
                    pool.wait_ge(*is_read(l, ("cb",)))
                pool.wait_ge(*exp_done.at(l, n + 1))
                i = SSD_GROUPS * c + q // 2
                s = s_sb[:, n % 2, :].rearrange("p (h k) -> p h k", k=P)
                pool.tensor_tensor(s, s, cbT[:, i:i + 1, :].to_broadcast([P, 4, P]), ALU.mult)\
                    .then_inc(weighed.sem, 1)

            with pool.Fori(0, DEPTH) as l:
                pool.wait_ge(*hi_ready.at(l, 1))
                for t in range(TT):
                    pool.wait_ge(*sq_done.at(l, t + 1))
                    norm(0, t, t + 1, pool_steps.at(l, 2 * t + 1), pool_steps.at(l, 2 * t + 2), rstd_done.sem)
                    if t == 0:
                        pool.wait_ge(*hi_ready.at(l, 1))
                        pool.tensor_tensor(w_lo[:, 0, 0:CUT], raw[:, 0, 0:CUT], w_hi[:, 0, 0:CUT].bitcast(F32),
                                           ALU.subtract).then_inc(lo_first.sem, 1)
                pool.wait_ge(*decay_exp.at(l, 1))
                pool.wait_ge(*acs_stored.at(l, 16))
                pool.wait_ge(*is_read(l, ("xs", 1, 0)))
                pool.tensor_tensor(xdec[:].rearrange("p (h d) -> p h d", d=HD),
                                   xdt[:, 0, :].rearrange("p (h d) -> p h d", d=HD),
                                   wide(decay[:, 0, :], HD), ALU.mult).then_inc(xdec_ready.sem, 1)
                for c in range(4):
                    before = 4 + 2 * c
                    for n in ((16, 17, 18), (19, 20), (21, 22), (23,))[c]:
                        weigh(l, n)
                    pool.wait_ge(*ssd_sq.at(l, c + 1))
                    step(*pool_steps.at(l, before + 1), pool.tensor_tensor(sms[:], ssq[:], pool_c[:, 1, 0:1], ALU.mult))
                    step(*pool_steps.at(l, before + 2), pool.tensor_tensor(sms[:], sms[:], pool_c[:, 2, 0:1], ALU.add))
                    pool.wait_ge(*ssd_yn.at(l, c))
                    pool.tensor_tensor(srstd[:], sms[:], pool_c[:, 3, 0:1], ALU.pow).then_inc(ssd_rstd.sem, 1)
                for n in (1, 2, 3):
                    pool.wait_ge(*sq_done.at(l, 2 * n + 2))
                    norm(n, 0, TT, pool_steps.at(l, 11 + 2 * n), pool_steps.at(l, 12 + 2 * n),
                         rstd_done.sem)
            for t in range(TT):
                pool.wait_ge(sq_fin, t + 1)
                norm(4, t, t + 1, (ms_fin, 2 * t + 1), (ms_fin, 2 * t + 2), rstd_fin)

        NCONST = 17
        NPAR = 16 * 8

        @block.scalar
        def _(act):
            act.wait_ge(angle_ready, 1)
            act.activation(cos2[:, :, 0:32], cos2[:, :, 0:32], ACT.Sin).then_inc(sines_ready, 1)
            act.activation(sin2[:, :, 32:64], sin2[:, :, 32:64], ACT.Sin).then_inc(sines_ready, 1)

            def hi(l, u, part=None):
                w, slot = UNITS[u], u % RING
                n = w["kt"] * w["cols"]
                act.wait_ge(*raw_loaded[slot].at(l, 16 * sum(loads[slot:u + 1:RING])))
                act.wait_ge(*unit_done.at(l, prev_user(u) + 1))
                cut = {None: slice(0, n), 0: slice(0, n // 2), 1: slice(n // 2, n)}[part]
                ins = act.activation(w_hi[:, slot, cut], raw[:, slot, cut], ACT.Copy)
                if part != 0:
                    ins.then_inc(hi_ready.sem, 1)

            def square(n, t, src, done):
                waste = xdec[:, 512 * t:512 * (t + 1)] if n == 1 else tmp[:, t, :]
                act.activation(waste.bitcast(mybir.dt.bfloat16), src[:, t, :], ACT.Square,
                               accum_out=sq[:, n, t:t + 1]).then_inc(done, 1)

            def norm_gain_hi(l, n, banks=range(4)):
                dst = hm_hi if n == 1 else act_hi
                if n == 1:
                    act.wait_ge(*unit_done.at(l, U_MIX))
                if n == 2:
                    act.wait_ge(*unit_done.at(l, U_KX))
                for b in banks:
                    act.wait_ge(*is_full(l, ("norm", n, b)))
                    if n == 0:
                        for i in range(4):
                            k = 4 * (b % 2) + i
                            ins = act.activation(dst[:, k, (b // 2) * P:(b // 2 + 1) * P],
                                                 bank(("norm", n, b))[:, i * P:(i + 1) * P],
                                                 ACT.Copy, scale=par[:, PC_NORM[n] + k:PC_NORM[n] + k + 1])
                        ins.then_inc(norm_hi.sem, 1)
                        continue
                    for kk in range(2):
                        k = 2 * b + kk
                        ins = act.activation(dst[:, k, :], bank(("norm", n, b))[:, kk * SEQ:(kk + 1) * SEQ],
                                             ACT.Copy, scale=par[:, PC_NORM[n] + k:PC_NORM[n] + k + 1])
                    ins.then_inc(norm_hi.sem, 1)

            def out_of_bank(l, key, dst, src=None):
                src = bank(key) if src is None else src
                act.activation(dst, src, ACT.Copy).then_inc(free(key), 1)

            def two(ap):
                return ap.rearrange("p (k n) -> p k n", n=SEQ)

            def evacuate(l, u):
                w, j = UNITS[u], UNITS[u]["index"]
                kind = w["kind"]
                if not w["last"] or kind in ("qa", "kva", "branch_a", "branch_b", "branch_c", "mix",
                                             "co", "down"):
                    return
                if kind == "xbc":
                    act.wait_ge(*conv_done.at(l, j + 1))
                    act.activation(tmp[:, 1, :], tmp[:, 0, :], ACT.Tanh).then_inc(conv_tanh.sem, 1)
                    return
                if kind == "up":
                    act.wait_ge(*unit_done.at(l, u + 1))
                    if j >= 2:
                        act.wait_ge(*relu_l.at(l, j - 1))
                    else:
                        act.wait_ge(*sq_done.at(l, 7 + j))
                    act.activation(tmp[:, j % 2, :], bank((u, 0)), ACT.Relu).then_inc(free((u, 0)), 1)
                    act.wait_ge(*is_read(l, (u, 0)))
                    act.activation(relu_hi[:, (j // 2) % 2, 2 * (j % 2):2 * (j % 2) + 2, :], two(tmp[:, j % 2, :]),
                                   ACT.Square).then_inc(relu_h.sem, 1)
                    return
                act.wait_ge(*unit_done.at(l, u + 1))
                if kind == "qkb":
                    out_of_bank(l, (u, 0), qkT_b[:, 2 * j:2 * j + 2, :], two(bank((u, 0))))
                elif kind == "kx":
                    out_of_bank(l, (u, 0), k_xT[:, 2 * j:2 * j + 2, :], two(bank((u, 0))))
                elif kind == "qx":
                    out_of_bank(l, (u, 0), q_xT[:, 2 * j:2 * j + 2, :], two(bank((u, 0))))
                elif kind in ("vb", "vx"):
                    for t in range(TT if kind == "vb" else 1):
                        key = unit_bank(u, t)
                        dst = v_b[:, t, :] if kind == "vb" else v_x[:, t, 512 * j:512 * j + 512]
                        out_of_bank(l, key, dst)
                elif kind == "z":
                    act.wait_ge(*xbc_ready.at(l, 4 + j))
                    for t in range(TT):
                        if j == 1:
                            act.wait_ge(*is_read(l, unit_bank(U_Z[0], t)))
                        act.activation(tmp[:, t, :], bank(unit_bank(u, t)), ACT.Tanh, scale=0.5)\
                           .then_inc(z_tanh.sem, 1)
                elif kind == "gate":
                    branch, tile = w["col"] // D, (w["col"] % D) // P
                    if branch == 1:
                        act.wait_ge(*is_read(l, (U_BRA + 1, 1)))
                    if branch == 2:
                        act.wait_ge(*is_read(l, (U_BRB + 1, 1)))
                    for m in range(2):
                        b0 = PC_BGATE + branch * KT + tile + m
                        ins = act.activation(g_sb[:, tile + m, :], bank((u, 0))[:, m * SEQ:(m + 1) * SEQ],
                                             ACT.Tanh, bias=half[:, b0:b0 + 1], scale=0.5)
                    ins.then_inc(free((u, 0)), 1)

            def merged_hi(l, j):
                act.wait_ge(*mg_ready.at(l, j + 1))
                act.activation(act_hi[:, 2 * j:2 * j + 2, :], mg_sb[:, 2 * j:2 * j + 2, :], ACT.Copy, scale=0.5)\
                   .then_inc(mg_hi.sem, 1)

            def turned_probs(l, n):
                if not 0 <= n < 16:
                    return
                n_cols = 2 * (job_of(n)[1] + 1) * P
                act.wait_ge(*is_full(l, ("probsT", n)))
                if n >= 2:
                    act.wait_ge(*values_done.at(l, n - 1))
                out_of_bank(l, ("probsT", n), pT_sb[:, n % 2, 0:n_cols], bank(("probsT", n))[:, 0:n_cols])

            def exps(l, n):
                if not 0 <= n < NJOBS:
                    return
                branch, t, j = job_of(n)
                if branch == 2:
                    act.wait_ge(*decays_made.at(l, n - SSD_JOB0 + 1))
                    act.activation(s_sb[:, n % 2, :], s_sb[:, n % 2, :], ACT.Exp).then_inc(exp_done.sem, 1)
                    return
                act.wait_ge(*masked.at(l, n + 1))
                keys = (t + 1) * P
                for i in range(2):
                    h = HEADS * t + head_of(j, i)
                    s = s_sb[:, n % 2, i * 2 * P:i * 2 * P + keys]
                    ins = act.activation(s, s, ACT.Exp, bias=neg_max[:, branch, h:h + 1], scale=ATT_SCALE,
                                         accum_out=den[:, branch, h:h + 1])
                ins.then_inc(exp_done.sem, 1)
                if branch == 0 and j == 3:
                    act.wait_ge(*sink_arg.at(l, t + 1))
                    act.activation(sink_e[:], sink_e[:], ACT.Exp).then_inc(sink_exp.sem, 1)

            def close_scale(l, i):
                act.wait_ge(*ssd_rstd.at(l, i - 3))
                act.activation(y_tok[:], y_tok[:], ACT.Copy, scale=srstd[:]).then_inc(ssd_yn.sem, 1)

            def close_square(l, i):
                act.wait_ge(*ssd_y.at(l, i - 3))
                act.wait_ge(*ssd_rstd.at(l, i - 4))
                if i > 4:
                    act.wait_ge(*ssd_sq.at(l, i - 4))
                act.activation(xdec[:, 0:512], y_tok[:], ACT.Square, accum_out=ssq[:]).then_inc(ssd_sq.sem, 1)

            def close_hi_part(l, i):
                _, branch, t, g = CLOSINGS[i]
                src = bank(("closeT", i))
                act.wait_ge(*is_full(l, ("closeT", i)))
                if branch < 2:
                    dst = (ya_hi, yb_hi)[branch]
                    act.activation(dst[:, :, t * P:(t + 1) * P], src.rearrange("p (k n) -> p k n", n=P), ACT.Copy)\
                       .then_inc(close_hi.sem, 1)
                    return
                if i == 4:
                    act.wait_ge(*values_done.at(l, 16))
                for k in range(4):
                    c = PC_SSDN + 4 * g + k
                    ins = act.activation(yc_hi[:, 4 * g + k, t * P:(t + 1) * P], src[:, k * P:(k + 1) * P], ACT.Copy,
                                         scale=par[:, c:c + 1])
                ins.then_inc(close_hi.sem, 1)

            def cross_exps(l, h):
                act.wait_ge(*xmax_ready.at(l, h + 1))
                if h >= 2:
                    act.wait_ge(*is_full(l, ("xprobsT", h - 2)))
                act.wait_ge(*xprobs.at(l, h))
                for t in range(TT):
                    ins = act.activation(s_sb[:, h % 2, t * SEQ:(t + 1) * SEQ],
                                         bank(("xscore", h))[:, t * SEQ:(t + 1) * SEQ], ACT.Exp,
                                         bias=xmax[:, t:t + 1], scale=rstd[:, 2, t:t + 1],
                                         accum_out=xden[:, t:t + 1])
                ins.then_inc(free(("xscore", h)), 1)

            def cross_out_hi(l, h):
                act.wait_ge(*is_full(l, ("xvalues", h)))
                act.activation(o_hi[:, 2 * h:2 * h + 2, :], two(bank(("xvalues", h))), ACT.Copy)\
                   .then_inc(xo_hi.sem, 1)

            act.wait_ge(x_loaded, 16)
            act.wait_ge(cols_ready, 1)
            with act.Fori(0, DEPTH) as l:
                act.activation(par[:], cols[:, l, :], ACT.Copy).then_inc(par_ready.sem, 1)
                act.activation(half[:], cols[:, l, 0:PC_ROWS], ACT.Copy, scale=0.5).then_inc(par_ready.sem, 1)
                hi(l, 0)
                x_left(act, l, 0)
                square(0, 0, x_sb, sq_done.sem)
                hi(l, 1, 0)
                for t in range(TT):
                    act.wait_ge(*rstd_done.at(l, t + 1))
                    act.activation(h_tok[:, t, :], x_sb[:, t, :], ACT.Copy, scale=rstd[:, 0, t:t + 1])\
                       .then_inc(htok_done.sem, 1)
                    if t == 0:
                        act.wait_ge(*par_ready.at(l, 1))
                    norm_gain_hi(l, 0, (2 * t,))
                    if t == 0:
                        hi(l, 1, 1)
                    norm_gain_hi(l, 0, (2 * t + 1,))
                    if t == 0:
                        x_left(act, l, 1)
                        square(0, 1, x_sb, sq_done.sem)
                hi(l, 2)
                for u, w in enumerate(UNITS):
                    h = u - CROSS_SLOT0
                    for i in range(4, 8):
                        if u == CLOSE_SLOT[i] + 1:
                            close_scale(l, i)
                    if u == SWA_T_SLOT:
                        for i in range(3):
                            act.wait_ge(*is_full(l, ("qkT", i)))
                            out_of_bank(l, ("qkT", i), qkT_a[:, 2 * i:2 * i + 2, :], two(bank(("qkT", i))))
                    turned_probs(l, job_at(u - 1))
                    if u == CB_SLOT:
                        act.wait_ge(*is_full(l, ("cb",)))
                        out_of_bank(l, ("cb",), cbT[:].rearrange("p k n -> p (k n)"))
                    if u == BTOK_SLOT:
                        act.wait_ge(*is_full(l, ("btok",)))
                        out_of_bank(l, ("btok",), b_tok[:].rearrange("p k n -> p (k n)"), bank(("btok",))[:, 0:SEQ])
                    if u == STATES_SLOT:
                        for g in range(SSD_GROUPS):
                            act.wait_ge(*is_full(l, ("states", g)))
                            out_of_bank(l, ("states", g), states[:, g, :])
                    for i in range(8):
                        if u == CLOSE_SLOT[i] + 1:
                            close_hi_part(l, i)
                    if 0 <= h - 1 < X_HEADS:
                        act.wait_ge(*is_full(l, ("xprobsT", h - 1)))
                        out_of_bank(l, ("xprobsT", h - 1), pT_x[:, h - 1, :, :], two(bank(("xprobsT", h - 1))))
                    if w["kind"] == "xbc":
                        hi(l, u + RING)
                    if u in (U_CO + 2, U_CO + 3):
                        norm_gain_hi(l, 3, ((0, 1), (2, 3))[u - U_CO - 2])
                    evacuate(l, u)
                    if w["kind"] == "branch_c":
                        merged_hi(l, w["index"])
                    if u + RING < NU and w["kind"] != "xbc":
                        hi(l, u + RING)
                    if u == U_SWA:
                        act.wait_ge(*sp_arg.at(l, 1))
                        act.activation(sp[:, 1, :], sp[:, 0, :], ACT.Exp, scale=-1.0).then_inc(sp_exp.sem, 1)
                        act.activation(par[:, PC_EXPA:PC_DSKIP], cols[:, l, PC_EXPA:PC_DSKIP], ACT.Exp)\
                           .then_inc(a_exp.sem, 1)
                    if u == ACS_SLOT:
                        act.wait_ge(*decay_arg.at(l, 1))
                        act.activation(decay[:], decay[:], ACT.Exp).then_inc(decay_exp.sem, 1)
                    for i in range(4, 8):
                        if u == CLOSE_SLOT[i]:
                            close_square(l, i)
                    exps(l, job_at(u))
                    if 0 <= h < X_HEADS:
                        cross_exps(l, h)
                    for hh in {U_VX + 2: (0, 1), U_VX + 3: (2, 3)}.get(u, ()):
                        cross_out_hi(l, hh)
                    if u == MEM_SQUARE_SLOT:
                        act.wait_ge(*mem_loaded.at(l, 16))
                        act.wait_ge(*ssd_sq.at(l, 4))
                        for t in range(TT):
                            square(1, t, mem_sb, sq_done.sem)
                    for n in (1, 2):
                        if u == NORM_TURN_SLOT[n]:
                            norm_gain_hi(l, n)
                    if u == NORM_TURN_SLOT[2] or u == U_CO + 3:
                        for t in range(TT):
                            square(2 if u < U_CO else 3, t, x_sb, sq_done.sem)
            for t in range(TT):
                x_left(act, DEPTH, t)
                square(4, t, x_sb, sq_fin)

        @block.tensor
        def _(pe):
            pe.wait_ge(const_made, NCONST)
            pe.wait_ge(par_loaded, NPAR)
            for l in range(DEPTH):
                pe.transpose(psum[:, l, 0:PC_ROWS], rows[0:PC_ROWS, l, :], ident[0:PC_ROWS, 0:PC_ROWS])\
                  .then_inc(rows_turned, 1)
            pe.wait_ge(cols_ready, 1)

            operands = {"h": (act_hi, act_lo), "merged": (act_hi, act_lo), "hq": (act_hi, act_lo),
                        "hf": (act_hi, act_lo), "mem": (hm_hi, hm_lo), "o": (o_hi, o_lo),
                        "y_swa": (ya_hi, ya_lo), "y_moba": (yb_hi, yb_lo), "y_ssd": (yc_hi, yc_lo)}

            def operand_ready(l, u):
                w = UNITS[u]
                act, j = w["act"], w["index"]
                if act == "relu":
                    pe.wait_ge(*relu_l.at(l, 2 * (j // 2) + 2))
                elif act == "merged":
                    pe.wait_ge(*mg_lo.at(l, 2 if w["first"] else 4))
                elif u > 0 and UNITS[u - 1]["act"] == act and (u != U_CO + 1):
                    return
                elif act == "mem":
                    wait_read(pe, l, [("norm", 1, b) for b in range(4)])
                elif act in ("h", "hq", "hf"):
                    return
                elif act == "o":
                    wait_read(pe, l, [("xvalues", h) for h in ((0, 1) if w["first"] else (2, 3))])
                else:
                    pe.wait_ge(*is_read(l, ("closeT", {"y_swa": 1, "y_moba": 3, "y_ssd": 7}[act])))

            def unit(l, u, tiles=range(TT)):
                w, slot = UNITS[u], u % RING
                kt, n = w["kt"], w["cols"]
                wait_lo(pe, l, u)
                operand_ready(l, u)
                if u < 2:
                    pe.wait_ge(*is_read(l, ("norm", 0, 2 * tiles[0] + u)))
                turned = {U_QX: 2, U_UP: 3}.get(u)
                if w["first"]:
                    for t, key in enumerate(unit_banks(u, w)):
                        if w["orient"] == "A" or t in tiles:
                            pe.wait_ge(*is_free(l, key))
                if w["act"] == "relu":
                    a_hi, a_lo = relu_hi[:, (w["index"] // 2) % 2], relu_lo[:, (w["index"] // 2) % 2]
                else:
                    a_hi, a_lo = operands[w["act"]][0][:], operands[w["act"]][1][:]
                m_hi = w_hi[:, slot, 0:kt * n].rearrange("p (k n) -> p k n", n=n)
                m_lo = w_lo[:, slot, 0:kt * n].rearrange("p (k n) -> p k n", n=n)
                k0 = w["row"] // P if w["act"] != "relu" else 0
                if w["orient"] == "A":
                    for m in range(n // P):
                        dst = bank(unit_banks(u, w)[m // 2])[:, (m % 2) * SEQ:(m % 2 + 1) * SEQ]
                        for k in range(kt):
                            if turned and m == 0 and k % 2 == 0:
                                pe.wait_ge(*is_read(l, ("norm", turned, k // 2)))
                            cs = slice(m * P, (m + 1) * P)
                            pe.matmul(dst, m_hi[:, k, cs], a_hi[:, k, :], start=k == 0, stop=False)
                            pe.matmul(dst, m_hi[:, k, cs], a_lo[:, k, :], start=False, stop=False)
                            ins = pe.matmul(dst, m_lo[:, k, cs], a_hi[:, k, :], start=False, stop=k == kt - 1)
                else:
                    for t in tiles:
                        dst = bank(unit_bank(u, t))[:, 0:n]
                        for k in range(kt):
                            first, last = w["first"] and k == 0, w["last"] and k == kt - 1
                            ts = slice(t * P, (t + 1) * P)
                            pe.matmul(dst, a_hi[:, k0 + k, ts], m_hi[:, k, :], start=first, stop=False)
                            pe.matmul(dst, a_hi[:, k0 + k, ts], m_lo[:, k, :], start=False, stop=False)
                            ins = pe.matmul(dst, a_lo[:, k0 + k, ts], m_hi[:, k, :], start=False, stop=last)
                if TT - 1 in tiles:
                    ins.then_inc(unit_done.sem, 1)
                elif u - 1 in PAIRS:
                    ins.then_inc(tile0_done.sem, 1)

            def norm0_turn(l, t):
                pe.wait_ge(*htok_done.at(l, t + 1))
                for half in range(2):
                    key = ("norm", 0, 2 * t + half)
                    pe.wait_ge(*is_free(l, key))
                    for i in range(4):
                        k = 4 * half + i
                        ins = pe.transpose(bank(key)[:, i * P:(i + 1) * P], h_tok[:, t, k * P:(k + 1) * P], ident[:])
                    ins.then_inc(full(key), 1)

            def norm_turn(l, n, banks=range(4)):
                src = mem_sb if n == 1 else x_sb
                for b in banks:
                    key = ("norm", n, b)
                    if n == 1 and b == 0:
                        pe.wait_ge(*mem_scaled.at(l, TT))
                    if n == 2 and b == 0:
                        wait_read(pe, l, [unit_bank(U_MIX + 1 + 2 * j, t) for j in range(2) for t in range(TT)])
                    if n == 3 and b in (0, 2):
                        wait_read(pe, l, [unit_bank(U_CO + 1 + b, t) for t in range(TT)])
                    pe.wait_ge(*is_free(l, key))
                    for kk in range(2):
                        for t in range(TT):
                            k = 2 * b + kk
                            ins = pe.transpose(bank(key)[:, kk * SEQ + t * P:kk * SEQ + (t + 1) * P],
                                               src[:, t, k * P:(k + 1) * P], ident[:])
                    ins.then_inc(full(key), 1)

            def swa_turn(l):
                pe.wait_ge(*roped.at(l, 4))
                for i in range(3):
                    key = ("qkT", i)
                    pe.wait_ge(*is_free(l, key))
                    for kk in range(2):
                        for t in range(TT):
                            k = 2 * i + kk
                            ins = pe.transpose(bank(key)[:, kk * SEQ + t * P:kk * SEQ + (t + 1) * P],
                                               qk_tok[:, t, k * P:(k + 1) * P], ident[:])
                    ins.then_inc(full(key), 1)

            def job_scores(l, n):
                branch, t, j = job_of(n)
                key = ("score", n)
                if n == 0:
                    wait_read(pe, l, [("qkT", i) for i in range(1, 3)])
                if n == 8:
                    wait_read(pe, l, [(first_of("qkb", i), 0) for i in range(4)] + [unit_bank(U_VB, t) for t in range(TT)])
                pe.wait_ge(*is_free(l, key))
                qk = (qkT_a, qkT_b)[branch]
                half_p = slice((j % 2) * HD, (j % 2 + 1) * HD)
                for i in range(2):
                    q_tile = head_of(j, i) // 2
                    k_tile = 4 + (j // 2 if branch == 0 else q_tile)
                    ins = pe.matmul(bank(key)[:, i * 2 * P:i * 2 * P + (t + 1) * P],
                                    qk[half_p, q_tile, t * P:(t + 1) * P], qk[half_p, k_tile, 0:(t + 1) * P],
                                    start=True, stop=True)
                ins.then_inc(full(key), 1)

            def job_turn(l, n):
                branch, t, j = job_of(n)
                key = ("probsT", n)
                pe.wait_ge(*exp_done.at(l, n + 1))
                pe.wait_ge(*is_free(l, key))
                for i in range(2):
                    for k in range(t + 1):
                        c = (i * (t + 1) + k) * P
                        ins = pe.transpose(bank(key)[:, c:c + P], s_sb[:, n % 2, i * 2 * P + k * P:i * 2 * P + (k + 1) * P],
                                           ident[:])
                ins.then_inc(full(key), 1)

            def job_values(l, n):
                branch, t, j = job_of(n)
                if branch < 2:
                    opens = n - j
                    pe.wait_ge(*is_read(l, ("probsT", n)))
                else:
                    opens = n - j % 2
                    pe.wait_ge(*weighed.at(l, n - 15))
                    if n == 16:
                        wait_read(pe, l, [("xs", 1, 0), ("xs", 1, 1)])
                key = ("values", opens)
                if n == opens:
                    pe.wait_ge(*is_free(l, key))
                if branch == 2:
                    for i in range(4):
                        c = (4 * (j % 2) + i) * HD
                        ins = pe.matmul(bank(key)[:, c:c + HD], s_sb[:, n % 2, i * P:(i + 1) * P],
                                        xdt[:, t, (4 * j + i) * HD:(4 * j + i + 1) * HD], start=True, stop=True)
                else:
                    for i in range(2):
                        hs = slice(head_of(j, i) * HD, (head_of(j, i) + 1) * HD)
                        for k in range(t + 1):
                            v = v_a[:, k, (j // 2) * HD:(j // 2 + 1) * HD] if branch == 0 else v_b[:, k, hs]
                            c = (i * (t + 1) + k) * P
                            ins = pe.matmul(bank(key)[:, hs],
                                            pT_sb[:, n % 2, c:c + P], v, start=k == 0, stop=k == t)
                ins.then_inc(values_done.sem, 1)

            def close_turn(l, i):
                job, branch = CLOSINGS[i][:2]
                key = ("closeT", i)
                if branch < 2:
                    pe.wait_ge(*is_read(l, ("values", job - 3)))
                else:
                    pe.wait_ge(*ssd_yn.at(l, i - 3))
                pe.wait_ge(*is_free(l, key))
                for k in range(4):
                    ins = pe.transpose(bank(key)[:, k * P:(k + 1) * P], y_tok[:, k * P:(k + 1) * P], ident[:])
                ins.then_inc(full(key), 1)

            def cross_scores(l, h):
                key = ("xscore", h)
                wait_read(pe, l, ([(U_KX + i, 0) for i in range(4)] if h == 0 else []) + [(U_QX + h, 0)])
                pe.wait_ge(*is_free(l, key))
                for t in range(TT):
                    for kk in range(2):
                        ins = pe.matmul(bank(key)[:, t * SEQ:(t + 1) * SEQ], q_xT[:, 2 * h + kk, t * P:(t + 1) * P],
                                        k_xT[:, 2 * h + kk, :], start=kk == 0, stop=kk == 1)
                ins.then_inc(full(key), 1)

            def cross_turn(l, h):
                key = ("xprobsT", h)
                pe.wait_ge(*xprobs.at(l, h + 1))
                pe.wait_ge(*is_free(l, key))
                for t in range(TT):
                    for m in range(2):
                        ins = pe.transpose(bank(key)[:, m * SEQ + t * P:m * SEQ + (t + 1) * P],
                                           s_sb[:, h % 2, t * SEQ + m * P:t * SEQ + (m + 1) * P], ident[:])
                ins.then_inc(full(key), 1)

            def cross_values(l, h):
                key = ("xvalues", h)
                for t in range(TT):
                    pe.wait_ge(*is_read(l, unit_bank(U_VX + 1 + 2 * (h // 2), t)))
                pe.wait_ge(*is_read(l, ("xprobsT", h)))
                pe.wait_ge(*is_free(l, key))
                for dd in range(2):
                    for m in range(2):
                        c = h * SEQ + dd * P
                        ins = pe.matmul(bank(key)[:, dd * SEQ:(dd + 1) * SEQ], v_x[:, m, c:c + P], pT_x[:, h, m, :],
                                        start=m == 0, stop=m == 1)
                ins.then_inc(full(key), 1)

            with pe.Fori(0, DEPTH) as l:
                for u in range(NU):
                    if u in PAIRS:
                        if u == U_QA:
                            norm0_turn(l, 0)
                        for t in range(TT):
                            if u == U_CO + 2 and t == 1:
                                norm_turn(l, 3, (0, 1))
                            unit(l, u, (t,))
                            if u == U_QA and t == 0:
                                norm0_turn(l, 1)
                            unit(l, u + 1, (t,))
                        if u == U_CO + 2:
                            norm_turn(l, 3, (2, 3))
                    elif u - 1 not in PAIRS:
                        unit(l, u)
                    h = u - CROSS_SLOT0
                    if u == SWA_T_SLOT:
                        swa_turn(l)
                    if 0 <= job_at(u) < SSD_JOB0:
                        job_scores(l, job_at(u))
                    if 0 <= job_at(u - 1) < SSD_JOB0:
                        job_turn(l, job_at(u - 1))
                    for i, (_, branch, c, g) in enumerate(CLOSINGS):
                        if branch == 2 and c == 1 and u == CLOSE_SLOT[i]:
                            key = ("yoff", g)
                            if g == 1:
                                pe.wait_ge(*is_read(l, ("states", 1)))
                            pe.wait_ge(*is_free(l, key))
                            pe.matmul(bank(key), xbcT[:, 10 + g, P:2 * P], states[:, g, :],
                                      start=True, stop=True).then_inc(full(key), 1)
                    if 0 <= job_at(u - 2):
                        job_values(l, job_at(u - 2))
                    if u == ACS_SLOT:
                        pe.wait_ge(*adt_ready.at(l, 1))
                        pe.wait_ge(*is_free(l, ("acs",)))
                        dst = bank(("acs",))
                        pe.matmul(dst[:, 0:2 * SSD_HEADS], tri[:], a_dt[:].rearrange("p t h -> p (t h)"),
                                  start=True, stop=True)
                        pe.matmul(dst[:, 2 * SSD_HEADS:3 * SSD_HEADS], ones[:], a_dt[:, 0, :],
                                  start=True, stop=True)
                        for t in range(TT):
                            ins = pe.matmul(dst[0:SSD_HEADS, (t + 1) * P:(t + 2) * P], a_dt[:, t, :], tri[:],
                                            start=True, stop=True)
                        ins.then_inc(full(("acs",)), 1)
                    if u == CB_SLOT:
                        pe.wait_ge(*xbc_ready.at(l, 6))
                        pe.wait_ge(*is_free(l, ("cb",)))
                        for c in range(TT):
                            for g in range(SSD_GROUPS):
                                i = SSD_GROUPS * c + g
                                ins = pe.matmul(bank(("cb",))[:, i * P:(i + 1) * P], xbcT[:, 8 + g, c * P:(c + 1) * P],
                                                xbcT[:, 10 + g, c * P:(c + 1) * P], start=True, stop=True)
                        ins.then_inc(full(("cb",)), 1)
                    if u == BTOK_SLOT:
                        pe.wait_ge(*xbc_ready.at(l, 5))
                        pe.wait_ge(*is_free(l, ("btok",)))
                        for g in range(SSD_GROUPS):
                            ins = pe.transpose(bank(("btok",))[:, g * P:(g + 1) * P], xbcT[:, 8 + g, 0:P], ident[:])
                        ins.then_inc(full(("btok",)), 1)
                    if u in XS_SLOTS:
                        g = XS_SLOTS.index(u)
                        pe.wait_ge(*xbc_ready.at(l, 4))
                        for t in range(TT):
                            key = ("xs", g, t)
                            pe.wait_ge(*is_free(l, key))
                            for k in range(4):
                                ins = pe.transpose(bank(key)[:, k * P:(k + 1) * P],
                                                   xbcT[:, 4 * g + k, t * P:(t + 1) * P], ident[:])
                            ins.then_inc(full(key), 1)
                    if u == STATES_SLOT:
                        pe.wait_ge(*xdec_ready.at(l, 1))
                        for g in range(SSD_GROUPS):
                            key = ("states", g)
                            pe.wait_ge(*is_free(l, key))
                            pe.matmul(bank(key), b_tok[:, g, :], xdec[:, 512 * g:512 * (g + 1)],
                                      start=True, stop=True).then_inc(full(key), 1)
                    for i in range(8):
                        if u == CLOSE_SLOT[i] + 1:
                            close_turn(l, i)
                    if 0 <= h < X_HEADS:
                        cross_scores(l, h)
                    if 0 <= h - 1 < X_HEADS:
                        cross_turn(l, h - 1)
                    for hh in {U_VX + 2: (0, 1), U_VX + 3: (2, 3)}.get(u, ()):
                        cross_values(l, hh)
                    for n in (1, 2):
                        if u == NORM_TURN_SLOT[n]:
                            norm_turn(l, n)

        @block.vector
        def _(dve):
            steps = Steps(dve, dve_steps, DVE_STEPS)
            TWO_PI = 2.0 * math.pi
            PI_PARTS = (6.28125, 0.0019350051879882812, TWO_PI - 6.28125 - 0.0019350051879882812)
            ROUND = 1.5 * 2.0 ** 23

            dve.wait_ge(pos_loaded, 32)
            steps.link(dve.tensor_copy(pos_f[:], pos_i[:]))
            turns = tmp[:, 0, 0:64].rearrange("p (t n) -> p t n", n=32)
            angle = tmp[:, 0, 64:128].rearrange("p (t n) -> p t n", n=32)
            for t in range(TT):
                steps.mark(dve.tensor_scalar(angle[:, t, :], inv_f[:], pos_f[:, t:t + 1], None, ALU.mult))
            steps.settle()
            for shift, dst in ((0.25, cos2[:, :, 0:32]), (0.0, sin2[:, :, 32:64])):
                steps.link(dve.tensor_scalar(turns, angle, 1.0 / TWO_PI, shift, ALU.mult, ALU.add))
                steps.link(dve.tensor_scalar(turns, turns, ROUND, None, ALU.add))
                steps.link(dve.tensor_scalar(turns, turns, ROUND, None, ALU.subtract))
                src = angle
                for part in PI_PARTS:
                    steps.link(dve.scalar_tensor_tensor(dst, turns, -part, src, ALU.mult, ALU.add))
                    src = dst
                steps.link(dve.tensor_scalar(dst, dst, shift * TWO_PI, 3.1415925, ALU.add, ALU.min))
                ins = dve.tensor_scalar(dst, dst, -3.1415925, None, ALU.max)
                if shift:
                    steps.link(ins)
                else:
                    ins.then_inc(angle_ready, 1)
            dve.wait_ge(sines_ready, 2)
            steps.mark(dve.tensor_copy(cos2[:, :, 32:64], cos2[:, :, 0:32]))
            steps.mark(dve.tensor_scalar(sin2[:, :, 0:32], sin2[:, :, 32:64], -1.0, None, ALU.mult))
            steps.settle()
            dve.wait_ge(rows_turned, DEPTH)
            for l in range(DEPTH):
                steps.mark(dve.tensor_copy(cols[:, l, 0:PC_ROWS], psum[:, l, 0:PC_ROWS]))
            dve.wait_ge(heads_loaded, 16 * 4)
            dve.tensor_scalar(cols[:, :, PC_SINK:PC_ALL], cols[:, :, PC_SINK:PC_ALL], 1.0 / ATT_SCALE, None,
                              ALU.mult).then_inc(cols_ready, 1)
            steps.settle()
            dve.wait_ge(cols_ready, 1)

            dve.wait_ge(x_loaded, 16)
            dve.wait_ge(const_made, NCONST)

            def lo(l, u):
                slot, n = u % RING, UNITS[u]["kt"] * UNITS[u]["cols"]
                dve.wait_ge(*hi_ready.at(l, u + 1))
                dve.tensor_tensor(w_lo[:, slot, 0:n], raw[:, slot, 0:n], w_hi[:, slot, 0:n].bitcast(F32),
                                  ALU.subtract).then_inc(lo_ready.sem, 1)

            def two(ap):
                return ap.rearrange("p (k n) -> p k n", n=SEQ)

            def mem_scale(l):
                dve.wait_ge(*rstd_done.at(l, 3))
                for t in range(TT):
                    dve.tensor_scalar(mem_sb[:, t, :], mem_sb[:, t, :], rstd[:, 1, t:t + 1], None, ALU.mult)\
                       .then_inc(mem_scaled.sem, 1)

            def norm_gain_lo(l, n, banks=range(4)):
                dst_hi, dst_lo = (hm_hi, hm_lo) if n == 1 else (act_hi, act_lo)
                for b in banks:
                    key = ("norm", n, b)
                    dve.wait_ge(*norm_hi.at(l, 4 * n + b + 1))
                    if n == 0:
                        for i in range(4):
                            k, ts = 4 * (b % 2) + i, slice((b // 2) * P, (b // 2 + 1) * P)
                            c = PC_NORM[n] + k
                            ins = dve.scalar_tensor_tensor(dst_lo[:, k, ts], bank(key)[:, i * P:(i + 1) * P],
                                                           par[:, c:c + 1], dst_hi[:, k, ts].bitcast(F32),
                                                           ALU.mult, ALU.subtract)
                        ins.then_inc(free(key), 1)
                        continue
                    for kk in range(2):
                        k = 2 * b + kk
                        c = PC_NORM[n] + k
                        ins = dve.scalar_tensor_tensor(dst_lo[:, k, :], bank(key)[:, kk * SEQ:(kk + 1) * SEQ],
                                                       par[:, c:c + 1], dst_hi[:, k, :].bitcast(F32),
                                                       ALU.mult, ALU.subtract)
                    ins.then_inc(free(key), 1)

            def rope(l, key, src, n_heads, t, dst, copies):
                shape = [P, n_heads, HD]
                src = src.rearrange("p (h d) -> p h d", d=HD)
                a0 = tmp[:, 0, 0:n_heads * HD].rearrange("p (h d) -> p h d", d=HD)
                a1 = tmp[:, 1, 0:n_heads * HD].rearrange("p (h d) -> p h d", d=HD)
                hf = HD // 2
                half_shape = [P, n_heads, hf]
                steps.mark(dve.tensor_tensor(a0, src, cos2[:, t:t + 1, :].to_broadcast(shape), ALU.mult))
                steps.mark(dve.tensor_tensor(a1[:, :, 0:hf], src[:, :, hf:HD],
                                             sin2[:, t:t + 1, 0:hf].to_broadcast(half_shape), ALU.mult))
                steps.mark(dve.tensor_tensor(a1[:, :, hf:HD], src[:, :, 0:hf],
                                             sin2[:, t:t + 1, hf:HD].to_broadcast(half_shape), ALU.mult))
                steps.settle()
                if copies == 1:
                    dve.tensor_tensor(dst.rearrange("p (h d) -> p h d", d=HD), a0, a1, ALU.add)\
                       .then_inc(roped.sem, 1)
                    return
                dst = dst.rearrange("p (h c d) -> p h c d", c=copies, d=HD)
                steps.mark(dve.tensor_tensor(dst[:, :, 0, :], a0, a1, ALU.add))
                dve.tensor_tensor(dst[:, :, 1, :], a0, a1, ALU.add).then_inc(roped.sem, 1)

            def softplus_dt(l):
                shape = [P, TT, SSD_HEADS]
                row = [sp[:, i, :] for i in range(6)]
                dve.wait_ge(*sp_arg.at(l, 1))
                steps.link(dve.tensor_scalar(row[2], row[2], 0.0, None, ALU.max))
                dve.wait_ge(*sp_exp.at(l, 1))
                steps.link(dve.tensor_scalar(row[3], row[1], 2.0, None, ALU.add))
                steps.link(dve.reciprocal(row[4], row[3]))
                steps.link(dve.tensor_tensor(row[3], row[1], row[4], ALU.mult))
                steps.link(dve.tensor_tensor(row[4], row[3], row[3], ALU.mult))
                steps.link(dve.tensor_scalar(row[5], row[4], 1.0 / 17.0, None, ALU.mult))
                for c in (15.0, 13.0, 11.0, 9.0, 7.0, 5.0, 3.0):
                    steps.link(dve.scalar_tensor_tensor(row[5], row[5], 1.0 / c, row[4], ALU.add, ALU.mult))
                steps.link(dve.scalar_tensor_tensor(row[5], row[5], 1.0, row[3], ALU.add, ALU.mult))
                dt_row = dt_sb[:].rearrange("p t h -> p (t h)")
                steps.link(dve.scalar_tensor_tensor(dt_row, row[5], 2.0, row[2], ALU.mult, ALU.add))
                dve.wait_ge(*a_exp.at(l, 1))
                dve.scalar_tensor_tensor(a_dt[:], dt_sb[:], -1.0,
                                         par[:, PC_EXPA:PC_DSKIP].unsqueeze(1).to_broadcast(shape),
                                         ALU.mult, ALU.mult).then_inc(adt_ready.sem, 1)

            def conv(l, u, j):
                key = (u, 0)
                y, x = two(tmp[:, 0, :]), two(bank(key))
                if j >= 4:
                    wait_read(dve, l, [unit_bank(U_Z[j - 4], t) for t in range(TT)])
                for tap in (3, 2, 1, 0):
                    s = 3 - tap
                    for m in range(2):
                        wc = PC_CONVW + 12 * tap + 2 * j + m
                        wcol, bcol = half[:, wc:wc + 1], half[:, PC_CONVB + 2 * j + m:PC_CONVB + 2 * j + m + 1]
                        if tap == 3:
                            ins = dve.tensor_scalar(y[:, m, :], x[:, m, :], wcol, bcol, ALU.mult, ALU.add)
                        else:
                            ins = dve.scalar_tensor_tensor(y[:, m, s:SEQ], x[:, m, 0:SEQ - s], wcol, y[:, m, s:SEQ],
                                                           ALU.mult, ALU.add)
                        if tap or not m:
                            steps.mark(ins)
                    if tap:
                        steps.settle()
                ins.then_inc(conv_done.sem, 1)
                dve.tensor_copy(mark_sb[:, 0:1], x[:, 0, 0:1]).then_inc(free(key), 1)
                lo(l, u + RING)
                dve.wait_ge(*conv_tanh.at(l, j + 1))
                steps.settle()
                dve.wait_ge(*conv_done.at(l, j + 1))
                dve.scalar_tensor_tensor(xbcT[:, 2 * j:2 * j + 2, :], two(tmp[:, 1, :]), 1.0, y, ALU.add, ALU.mult)\
                   .then_inc(xbc_ready.sem, 1)

            def add_to_x(key, t, j):
                xs = x_sb[:, t, 512 * j:512 * j + 512]
                dve.tensor_tensor(xs, xs, bank(key), ALU.add).then_inc(free(key), 1)

            def evacuate(l, u):
                w, j = UNITS[u], UNITS[u]["index"]
                kind = w["kind"]
                if u == U_CO + 2:
                    dve.wait_ge(*tile0_done.at(l, 2))
                    add_to_x(unit_bank(u, 0), 0, 1)
                    return
                if kind == "down":
                    if u < NU - 2:
                        return
                    t = u - (NU - 2)
                    if t == 0:
                        dve.wait_ge(*rstd_done.at(l, 5))
                        dve.wait_ge(*tile0_done.at(l, 3))
                    for jj in range(2):
                        if t == 1:
                            dve.wait_ge(*unit_done.at(l, NU - 1 + jj))
                        key, xs = ("down", 2 * jj + t), x_sb[:, t, 512 * jj:512 * jj + 512]
                        dve.scalar_tensor_tensor(xs, bank(key), rstd[:, 3, t:t + 1], xs, ALU.mult, ALU.add)\
                           .then_inc(free(key), 1)
                    return
                if not w["last"] or kind in ("qkb", "vb", "kx", "qx", "gate"):
                    return
                dve.wait_ge(*unit_done.at(l, u + 1))
                if kind == "vx":
                    key = unit_bank(u, 1)
                    dve.tensor_copy(v_x[:, 1, 512 * j:512 * j + 512], bank(key)).then_inc(free(key), 1)
                    return
                if kind == "qa":
                    lo(l, u + RING)
                    for t in range(TT):
                        key = unit_bank(u, t)
                        rope(l, key, bank(key), HEADS, t, qk_tok[:, t, 0:512], 1)
                        dve.tensor_copy(mark_sb[:, 0:1], bank(key)[:, 0:1]).then_inc(free(key), 1)
                        steps.settle()
                        dve.wait_ge(*is_read(l, key))
                        dve.wait_ge(*roped.at(l, t + 1))
                elif kind == "kva":
                    for t in range(TT):
                        key = unit_bank(u, t)
                        src = bank(key)
                        steps.mark(dve.tensor_copy(v_a[:, t, :], src[:, P:SEQ]))
                        rope(l, key, src[:, 0:P], SWA_KV, t, qk_tok[:, t, 512:768], 2)
                        dve.tensor_tensor(sp[:, 2, t * SSD_HEADS:(t + 1) * SSD_HEADS],
                                          src[:, SEQ:SEQ + SSD_HEADS], par[:, PC_DTB:PC_DTB + SSD_HEADS], ALU.add)\
                           .then_inc(free(key), 1)
                        steps.settle()
                        dve.wait_ge(*roped.at(l, 3 + t))
                    wait_read(dve, l, [unit_bank(u, t) for t in range(TT)])
                    dve.scalar_tensor_tensor(sp[:, 0, :], sp[:, 2, :], -1.0, sp[:, 2, :], ALU.mult, ALU.max)\
                       .then_inc(sp_arg.sem, 1)
                elif kind == "xbc":
                    conv(l, u, j)
                elif kind == "z":
                    for t in range(TT):
                        key = unit_bank(u, t)
                        dve.wait_ge(*z_tanh.at(l, 2 * j + t + 1))
                        dve.scalar_tensor_tensor(z_sb[:, t, 512 * j:512 * j + 512], tmp[:, t, :], 1.0, bank(key),
                                                 ALU.add, ALU.mult).then_inc(free(key), 1)
                elif kind in ("branch_a", "branch_b", "branch_c"):
                    for i, key in enumerate(unit_banks(u, w)):
                        c = w["col"] // P + 2 * i
                        g, mg = g_sb[:, c:c + 2, :], mg_sb[:, c:c + 2, :]
                        if i == 0:
                            wait_read(dve, l, [(v, 0) for v in range(u - 8, u) if UNITS[v]["kind"] == "gate"])
                        if kind == "branch_a":
                            dve.scalar_tensor_tensor(mg, g, 1.0, two(bank(key)), ALU.add, ALU.mult)\
                               .then_inc(free(key), 1)
                            continue
                        part = two(tmp[:, i, :])
                        dve.scalar_tensor_tensor(part, g, 1.0, two(bank(key)), ALU.add, ALU.mult)\
                           .then_inc(free(key), 1)
                        dve.wait_ge(*is_read(l, key))
                        steps.settle()
                        ins = dve.tensor_tensor(mg, mg, part, ALU.add)
                        if kind == "branch_b":
                            steps.mark(ins)
                        else:
                            ins.then_inc(mg_ready.sem, 1)
                            dve.wait_ge(*mg_ready.at(l, j + 1))
                elif kind in ("mix", "co"):
                    for t in range(TT):
                        if u != U_CO + 3 or t == 1:
                            add_to_x(unit_bank(u, t), t, j)
                elif kind == "up":
                    dve.wait_ge(*is_read(l, (u, 0)))
                    steps.mark(dve.tensor_tensor(pT_sb[:, j % 2, :], tmp[:, j % 2, :], tmp[:, j % 2, :], ALU.mult))

            def merged_lo(l, j):
                dve.wait_ge(*mg_hi.at(l, j + 1))
                cs = slice(2 * j, 2 * j + 2)
                dve.scalar_tensor_tensor(act_lo[:, cs, :], mg_sb[:, cs, :], 0.5, act_hi[:, cs, :].bitcast(F32),
                                         ALU.mult, ALU.subtract).then_inc(mg_lo.sem, 1)

            def relu_low(l, j):
                steps.settle()
                dve.wait_ge(*relu_h.at(l, j + 1))
                f, m = (j // 2) % 2, slice(2 * (j % 2), 2 * (j % 2) + 2)
                dve.tensor_tensor(relu_lo[:, f, m, :], two(pT_sb[:, j % 2, :]), relu_hi[:, f, m, :].bitcast(F32),
                                  ALU.subtract).then_inc(relu_l.sem, 1)

            def job_mask(l, n):
                branch, t, j = job_of(n)
                key = ("score", n)
                if n < SSD_JOB0:
                    dve.wait_ge(*is_full(l, key))
                else:
                    dve.wait_ge(*acs_spread.at(l, 16 * (n - SSD_JOB0 + 1)))
                if 2 <= n < 18:
                    dve.wait_ge(*is_full(l, ("probsT", n - 2)))
                elif n >= 18:
                    dve.wait_ge(*values_done.at(l, n - 1))
                if branch == 2:
                    if n == 16:
                        dve.wait_ge(*decay_arg.at(l, 1))
                    for i in range(4):
                        h = 4 * j + i
                        ins = dve.scalar_tensor_tensor(s_sb[:, n % 2, i * P:(i + 1) * P],
                                                       pT_sb[:, n % 2, i * P:(i + 1) * P],
                                                       acs[:, t, h:h + 1], mask_ssd[:], ALU.subtract, ALU.min)
                    ins.then_inc(decays_made.sem, 1)
                    return
                dve.wait_ge(*masked.at(l, n))
                dve.memset(mark_sb[:, 1 + n:2 + n], 0.0)
                keys = (t + 1) * P
                mask = (mask_swa, mask_moba)[branch][:, 2 * P - keys:2 * P]
                for i in range(2):
                    c = i * 2 * P
                    ins = dve.tensor_tensor_reduce(s_sb[:, n % 2, c:c + keys], bank(key)[:, c:c + keys], mask, 1.0,
                                                   -3.0e38, ALU.add, ALU.max, row_max[:, i:i + 1])
                    if i == 0:
                        steps.mark(ins)
                ins.then_inc(free(key), 1)
                steps.settle()
                dve.wait_ge(*is_read(l, key))
                if branch == 0:
                    c = PC_SINK + head_of(j, 0)
                    steps.link(dve.tensor_tensor(row_max[:], row_max[:], par[:, c:c + 3:2], ALU.max))
                h = HEADS * t + head_of(j, 0)
                dve.tensor_scalar(neg_max[:, branch, h:h + 3:2], row_max[:], -ATT_SCALE, None, ALU.mult)\
                   .then_inc(masked.sem, 1)
                if branch == 0 and j == 3:
                    dve.wait_ge(*masked.at(l, n + 1))
                    dve.scalar_tensor_tensor(sink_e[:], par[:, PC_SINK:PC_ALL], ATT_SCALE,
                                             neg_max[:, 0, HEADS * t:HEADS * (t + 1)], ALU.mult, ALU.add)\
                       .then_inc(sink_arg.sem, 1)

            def close(l, i):
                job, branch, t, g = CLOSINGS[i]
                before = xd_sb[:, g, t, :] if branch == 2 else None
                if branch == 2 and t == 1:
                    key, before = ("yoff", g), tmp[:, 1, :]
                    steps.settle()
                    dve.wait_ge(*is_full(l, key))
                    dve.tensor_tensor(before.rearrange("p (h d) -> p h d", d=HD),
                                      bank(key).rearrange("p (h d) -> p h d", d=HD),
                                      wide(decay[:, 1, 8 * g:8 * g + 8], HD), ALU.mult).then_inc(free(key), 1)
                    dve.wait_ge(*is_read(l, key))
                    steps.link(dve.tensor_tensor(before, before, xd_sb[:, g, t, :], ALU.add))
                dve.wait_ge(*values_done.at(l, job + 1))
                if i:
                    dve.wait_ge(*is_full(l, ("closeT", i - 1)))
                y3 = y_tok[:].rearrange("p (h d) -> p h d", d=HD)
                if branch < 2:
                    key = ("values", job - 3)
                    src = bank(key).rearrange("p (h d) -> p h d", d=HD)
                    d = den[:, branch, HEADS * t:HEADS * (t + 1)]
                    if branch == 0:
                        dve.wait_ge(*sink_exp.at(l, t + 1))
                        steps.link(dve.tensor_tensor(d, d, sink_e[:], ALU.add))
                    steps.link(dve.reciprocal(rden[:], d))
                    dve.tensor_tensor(y3, src, wide(rden[:], HD), ALU.mult).then_inc(free(key), 1)
                    return
                key = ("values", job - 1)
                dve.tensor_tensor(y_tok[:], bank(key), before, ALU.add).then_inc(free(key), 1)
                dve.wait_ge(*is_read(l, key))
                dve.scalar_tensor_tensor(y_tok[:], y_tok[:], 0.5, z_sb[:, t, 512 * g:512 * (g + 1)],
                                         ALU.mult, ALU.mult).then_inc(ssd_y.sem, 1)

            def close_lo_part(l, i):
                _, branch, t, g = CLOSINGS[i]
                key = ("closeT", i)
                dve.wait_ge(*close_hi.at(l, i + 1))
                ts = slice(t * P, (t + 1) * P)
                if branch < 2:
                    d_hi, d_lo = ((ya_hi, ya_lo), (yb_hi, yb_lo))[branch]
                    dve.tensor_tensor(d_lo[:, :, ts], bank(key).rearrange("p (k n) -> p k n", n=P),
                                      d_hi[:, :, ts].bitcast(F32), ALU.subtract).then_inc(free(key), 1)
                    return
                for k in range(4):
                    c = PC_SSDN + 4 * g + k
                    ins = dve.scalar_tensor_tensor(yc_lo[:, 4 * g + k, ts], bank(key)[:, k * P:(k + 1) * P],
                                                   par[:, c:c + 1], yc_hi[:, 4 * g + k, ts].bitcast(F32),
                                                   ALU.mult, ALU.subtract)
                ins.then_inc(free(key), 1)

            def sums_of_adt(l):
                key = ("acs",)
                n = SSD_HEADS
                dve.wait_ge(*is_full(l, key))
                dve.tensor_copy(acsT[:], bank(key)[0:SSD_HEADS, P:P + SEQ]).then_inc(acs_turned.sem, 1)
                steps.link(dve.tensor_copy(acs[:].rearrange("p t h -> p (t h)"), bank(key)[:, 0:2 * n]))
                dve.tensor_tensor(decay[:, 0, :], bank(key)[:, 2 * n:3 * n], acs[:, 0, :], ALU.subtract)\
                   .then_inc(free(key), 1)
                dve.tensor_copy(decay[:, 1, :], acs[:, 1, :]).then_inc(decay_arg.sem, 1)

            def xs_tokens(l, g):
                if g == 0:
                    dve.wait_ge(*values_done.at(l, 8))
                for t in range(TT):
                    dve.wait_ge(*is_full(l, ("xs", g, t)))
                for t in range(TT):
                    key = ("xs", g, t)
                    src = bank(key).rearrange("p (h d) -> p h d", d=HD)
                    hs = slice(8 * g, 8 * g + 8)
                    steps.mark(dve.tensor_tensor(xdt[:, t, 512 * g:512 * (g + 1)].rearrange("p (h d) -> p h d", d=HD),
                                                 src, wide(dt_sb[:, t, hs], HD), ALU.mult))
                    dve.tensor_tensor(xd_sb[:, g, t, :].rearrange("p (h d) -> p h d", d=HD), src,
                                      wide(par[:, PC_DSKIP + 8 * g:PC_DSKIP + 8 * g + 8], HD), ALU.mult)\
                       .then_inc(free(key), 1)

            with dve.Fori(0, DEPTH) as l:
                steps.enter(l)
                dve.wait_ge(*par_ready.at(l, 2))
                dve.wait_ge(*hi_ready.at(l, 1))
                dve.tensor_tensor(w_lo[:, 0, CUT:2048], raw[:, 0, CUT:2048], w_hi[:, 0, CUT:2048].bitcast(F32),
                                  ALU.subtract).then_inc(lo_first.sem, 1)
                norm_gain_lo(l, 0, (0, 1))
                lo(l, 1)
                norm_gain_lo(l, 0, (2, 3))
                lo(l, 2)
                for u, w in enumerate(UNITS):
                    h = u - CROSS_SLOT0
                    if 0 <= job_at(u):
                        job_mask(l, job_at(u))
                    if u == ACS_SLOT:
                        sums_of_adt(l)
                    if u == DT_SLOT:
                        softplus_dt(l)
                    if u in XS_SLOTS:
                        xs_tokens(l, XS_SLOTS.index(u))
                    for i in range(8):
                        if u == CLOSE_SLOT[i] + 1:
                            close_lo_part(l, i)
                    for i in range(8):
                        if u == CLOSE_SLOT[i]:
                            close(l, i)
                    if 0 <= h < X_HEADS:
                        if h:
                            dve.wait_ge(*is_read(l, ("xscore", h - 1)))
                        dve.wait_ge(*is_full(l, ("xscore", h)))
                        steps.link(dve.tensor_reduce(xmax[:], two(bank(("xscore", h))), AX.X, ALU.max))
                        if h == 0:
                            dve.wait_ge(*rstd_done.at(l, 4))
                        dve.scalar_tensor_tensor(xmax[:], xmax[:], -1.0, rstd[:, 2, :], ALU.mult, ALU.mult)\
                           .then_inc(xmax_ready.sem, 1)
                    evacuate(l, u)
                    if u in (U_CO + 2, U_CO + 3):
                        norm_gain_lo(l, 3, ((0, 1), (2, 3))[u - U_CO - 2])
                    if w["kind"] == "branch_c":
                        merged_lo(l, w["index"])
                    if u == U_CO + 3:
                        lo(l, u + RING - 1)
                    if u + RING < NU and w["kind"] != "xbc" and u not in (U_QA + 1, U_CO + 2):
                        lo(l, u + RING)
                    if w["kind"] == "up":
                        relu_low(l, w["index"])
                    if 0 <= h < X_HEADS:
                        dve.wait_ge(*is_read(l, ("xscore", h)))
                        steps.link(dve.reciprocal(row_max[:], xden[:]))
                        for t in range(TT):
                            s = s_sb[:, h % 2, t * SEQ:(t + 1) * SEQ]
                            ins = dve.tensor_scalar(s, s, row_max[:, t:t + 1], None, ALU.mult)
                            if t == 0:
                                steps.mark(ins)
                        ins.then_inc(xprobs.sem, 1)
                    for hh in {U_VX + 2: (0, 1), U_VX + 3: (2, 3)}.get(u, ()):
                        dve.wait_ge(*xo_hi.at(l, hh + 1))
                        cs = slice(2 * hh, 2 * hh + 2)
                        dve.tensor_tensor(o_lo[:, cs, :], two(bank(("xvalues", hh))), o_hi[:, cs, :].bitcast(F32),
                                          ALU.subtract).then_inc(free(("xvalues", hh)), 1)
                    if u == MEM_SCALE_SLOT:
                        mem_scale(l)
                    for n in (1, 2):
                        if u == NORM_TURN_SLOT[n]:
                            norm_gain_lo(l, n)
                steps.leave(DEPTH)
            dve.wait_ge(gain_loaded, 16)
            for t in range(TT):
                dve.wait_ge(rstd_fin, t + 1)
                for cs in (slice(0, 512), slice(512, D)):
                    dve.scalar_tensor_tensor(h_tok[:, t, cs], x_sb[:, t, cs], rstd[:, 4, t:t + 1], gain[:, cs],
                                             ALU.mult, ALU.mult).then_inc(fin_ready, 1)


_INS = ["x", "mem", "positions", "norm_mix", "w_in", "w_gate", "b_gate", "swa_sinks", "conv_w", "conv_b", "dt_bias",
        "a_log", "d_skip", "ssd_norm", "w_br_swa", "w_br_moba", "w_br_ssd", "w_mix_out", "norm_cross", "norm_mem",
        "w_cq", "w_ckv", "w_co", "norm_mlp", "w_up", "w_down", "final_norm"]


def kernel(**inputs):
    import concourse.bacc as bacc
    from concourse.bass_utils import run_bass_kernel_spmd

    nc = bacc.Bacc("TRN2", target_bir_lowering=False, num_devices=1)
    arrays, args = {}, {}
    for name in _INS:
        arr = np.ascontiguousarray(inputs[name])
        arrays[f"in_{name}_dram"] = arr
        args[name] = nc.dram_tensor(f"in_{name}_dram", arr.shape, mybir.dt.from_np(arr.dtype),
                                    kind="ExternalInput").ap()
    out = nc.dram_tensor("out_0_dram", (1, SEQ, D), F32, kind="ExternalOutput").ap()
    trunk(nc, args, out)
    r = run_bass_kernel_spmd(nc, [arrays], core_ids=[0])
    return r.results[0]["out_0_dram"]
```
